# Optimizing a Trainium2 kernel written in Bass

```python
import math
import jax, jax.numpy as jnp
from jax import lax
import numpy as np

D_MODEL = 1024
BATCH = 1
SEQ = 256
DEPTH = 1
DEC_BATCH = 1
DEC_SEQ = 512
PAST_LEN = 128

MIX_WIDTH = D_MODEL
HG_HEADS = 4
HG_KEY_DIM = 128
HG_VAL_DIM = (MIX_WIDTH // 2) // HG_HEADS
HG_FWIDTH = HG_HEADS * HG_KEY_DIM
HG_WIDTH = HG_HEADS * HG_VAL_DIM
HG_CHUNK = 64
DA_HEADS = 4
DA_QK_DIM = 64
DA_VAL_DIM = 2 * DA_QK_DIM
DA_QK_WIDTH = DA_HEADS * 2 * DA_QK_DIM
DA_WIDTH = DA_HEADS * DA_VAL_DIM
ROT_DIM = DA_QK_DIM // 4
ROPE_THETA = 500000.0
Q_BLOCK = 128
N_EXPERTS = 16
CAPACITY_FACTOR = 2
D_FF = 2816
NORM_EPS = 1e-6
IN_WIDTHS = (HG_FWIDTH, HG_FWIDTH, HG_FWIDTH, HG_WIDTH, HG_WIDTH, DA_QK_WIDTH, DA_QK_WIDTH, DA_WIDTH)
IN_WIDTH = HG_FWIDTH * 3 + HG_WIDTH * 2 + DA_QK_WIDTH * 2 + DA_WIDTH

kernel_name = "hymba_hgrn2_diffattn_ec_moe_encoder"

def rms_norm(x, w):
    xf = x.astype(jnp.float32)
    y = xf * lax.rsqrt(jnp.mean(xf * xf, axis=-1, keepdims=True) + NORM_EPS)
    return (y * w.astype(jnp.float32)).astype(x.dtype)

def split_points():
    pts, acc = [], 0
    for w in IN_WIDTHS[:-1]:
        acc += w
        pts.append(acc)
    return tuple(pts)

def gla_chunkwise(q, k, g, v):
    B, T, H, K = q.shape
    V = v.shape[-1]
    N = T // HG_CHUNK

    def to_chunks(a):
        return a.reshape(B, N, HG_CHUNK, H, a.shape[-1]).transpose(1, 0, 2, 3, 4)

    qc, kc, gc, vc = to_chunks(q), to_chunks(k), to_chunks(g), to_chunks(v)
    bc = jnp.cumsum(gc, axis=2)
    causal = jnp.tril(jnp.ones((HG_CHUNK, HG_CHUNK), dtype=bool))[None, :, :, None, None]

    def step(S, inp):
        q_, k_, b_, v_ = inp
        o_inter = jnp.einsum('bihk,bhkv->bihv', q_ * jnp.exp(b_), S)
        rel = jnp.where(causal, b_[:, :, None] - b_[:, None, :], -jnp.inf)
        att = jnp.einsum('bihk,bjhk,bijhk->bhij', q_, k_, jnp.exp(rel))
        o_intra = jnp.einsum('bhij,bjhv->bihv', att, v_)
        b_last = b_[:, -1]
        k_dec = k_ * jnp.exp(b_last[:, None] - b_)
        S_new = jnp.exp(b_last)[..., None] * S + jnp.einsum('bjhk,bjhv->bhkv', k_dec, v_)
        return S_new, o_inter + o_intra

    S0 = jnp.zeros((B, H, K, V), jnp.float32)
    _, o = lax.scan(step, S0, (qc, kc, bc, vc))
    return o.transpose(1, 0, 2, 3, 4).reshape(B, T, H, V)

def hgrn2_bidirectional(hq, hf_f, hf_b, hi, hg, lb_f, lb_b, norm_w):
    B, T, _ = hq.shape
    f32 = jnp.float32
    q = jax.nn.silu(hq.astype(f32)).reshape(B, T, HG_HEADS, HG_KEY_DIM) * (HG_KEY_DIM ** -0.5)
    v = hi.astype(f32).reshape(B, T, HG_HEADS, HG_VAL_DIM)

    def gates(fr, lb):
        f = lb + (1.0 - lb) * jax.nn.sigmoid(fr.astype(f32).reshape(B, T, HG_HEADS, HG_KEY_DIM))
        return 1.0 - f, jnp.log(f)

    k_f, g_f = gates(hf_f, lb_f)
    k_b, g_b = gates(hf_b, lb_b)
    o_fwd = gla_chunkwise(q, k_f, g_f, v)
    o_bwd = jnp.flip(gla_chunkwise(jnp.flip(q, 1), jnp.flip(k_b, 1), jnp.flip(g_b, 1), jnp.flip(v, 1)), 1)
    gate = jax.nn.silu(hg.astype(f32).reshape(B, T, HG_HEADS, HG_VAL_DIM))
    o = rms_norm(o_fwd + o_bwd, norm_w) * gate
    return o.reshape(B, T, HG_WIDTH).astype(hq.dtype)

def rope_tables(T):
    inv_freq = 1.0 / (ROPE_THETA ** (jnp.arange(0, ROT_DIM, 2, dtype=jnp.float32) / ROT_DIM))
    ang = jnp.arange(T, dtype=jnp.float32)[:, None] * inv_freq[None, :]
    return jnp.cos(ang)[:, None, None, :], jnp.sin(ang)[:, None, None, :]

def apply_partial_rope(x, cos, sin):
    half = ROT_DIM // 2
    x1, x2, rest = x[..., :half], x[..., half:ROT_DIM], x[..., ROT_DIM:]
    c, s = cos.astype(x.dtype), sin.astype(x.dtype)
    return jnp.concatenate([x1 * c - x2 * s, x2 * c + x1 * s, rest], axis=-1)

def diff_attention(aq, ak, av, layer, q_norm_w, k_norm_w, lq1, lk1, lq2, lk2, subln_w):
    B, T, _ = aq.shape
    f32 = jnp.float32
    q = rms_norm(aq.reshape(B, T, DA_HEADS, 2, DA_QK_DIM), q_norm_w)
    k = rms_norm(ak.reshape(B, T, DA_HEADS, 2, DA_QK_DIM), k_norm_w)
    cos, sin = rope_tables(T)
    q = apply_partial_rope(q, cos, sin)
    k = apply_partial_rope(k, cos, sin)
    v32 = av.reshape(B, T, DA_HEADS, DA_VAL_DIM).astype(f32)
    lam_init = 0.8 - 0.6 * math.exp(-0.3 * layer)
    lam = (jnp.exp(jnp.sum(lq1.astype(f32) * lk1.astype(f32)))
           - jnp.exp(jnp.sum(lq2.astype(f32) * lk2.astype(f32))) + lam_init)
    scale = DA_QK_DIM ** -0.5
    nb = T // Q_BLOCK
    qb = q.reshape(B, nb, Q_BLOCK, DA_HEADS, 2, DA_QK_DIM).transpose(1, 0, 2, 3, 4, 5)

    def attend(q_blk):
        s = jnp.einsum('bqhcd,bkhcd->bhcqk', q_blk, k).astype(f32) * scale
        p = jax.nn.softmax(s, axis=-1)
        pd = p[:, :, 0] - lam * p[:, :, 1]
        return jnp.einsum('bhqk,bkhv->bqhv', pd, v32)

    o = lax.map(attend, qb)
    o = o.transpose(1, 0, 2, 3, 4).reshape(B, T, DA_HEADS, DA_VAL_DIM)
    o = rms_norm(o, subln_w) * (1.0 - lam_init)
    return o.reshape(B, T, DA_WIDTH).astype(aq.dtype)

def expert_choice_moe(h, router_w, w1, w3, w2):
    B, T, D = h.shape
    n = B * T
    cap = CAPACITY_FACTOR * n // N_EXPERTS
    xt = h.reshape(n, D)
    aff = jax.nn.softmax((xt @ router_w).astype(jnp.float32), axis=-1)
    gates, idx = lax.top_k(aff.T, cap)

    def expert(args):
        w1e, w3e, w2e, ie, ge = args
        xe = jnp.take(xt, ie, axis=0)
        hid = jax.nn.silu(xe @ w1e) * (xe @ w3e)
        return (hid @ w2e).astype(jnp.float32) * ge[:, None]

    ye = lax.map(expert, (w1, w3, w2, idx, gates))
    out = jnp.zeros((n, D), jnp.float32).at[idx.reshape(-1)].add(ye.reshape(-1, D))
    return out.reshape(B, T, D).astype(h.dtype)

def hybrid_layer(x, layer, norm1_w, w_in, lb_f, lb_b, hg_norm_w, q_norm_w, k_norm_w,
                 lq1, lk1, lq2, lk2, subln_w, w_out, norm2_w, router_w, w1, w3, w2):
    xn = rms_norm(x, norm1_w)
    proj = xn @ w_in
    hq, hf_f, hf_b, hi, hg, aq, ak, av = jnp.split(proj, split_points(), axis=-1)
    o_hg = hgrn2_bidirectional(hq, hf_f, hf_b, hi, hg, lb_f, lb_b, hg_norm_w)
    o_da = diff_attention(aq, ak, av, layer, q_norm_w, k_norm_w, lq1, lk1, lq2, lk2, subln_w)
    h = x + (jnp.concatenate([o_hg, o_da], axis=-1) @ w_out).astype(x.dtype)
    return h + expert_choice_moe(rms_norm(h, norm2_w), router_w, w1, w3, w2)

def setup_inputs(seed: int = 0) -> dict:
    key = jax.random.key(seed)
    ks = jax.random.split(key, 20)

    def nrm(k, shape, scale):
        return jax.random.normal(k, shape, jnp.float32) * scale

    def gain(k, shape):
        return 1.0 + 0.02 * jax.random.normal(k, shape, jnp.float32)

    return {
        "x_prompt": nrm(ks[0], (BATCH, SEQ, D_MODEL), 1.0),
        "x_sample": nrm(ks[1], (DEC_BATCH, DEC_SEQ, D_MODEL), 1.0),
        "norm1_w": gain(ks[2], (DEPTH, D_MODEL)),
        "w_in": nrm(ks[3], (DEPTH, D_MODEL, IN_WIDTH), D_MODEL ** -0.5),
        "hg_lb_fwd": nrm(ks[4], (DEPTH + 1, HG_FWIDTH), 0.1),
        "hg_lb_bwd": nrm(ks[5], (DEPTH + 1, HG_FWIDTH), 0.1),
        "hg_norm_w": gain(ks[6], (DEPTH, HG_VAL_DIM)),
        "q_norm_w": gain(ks[7], (DEPTH, DA_QK_DIM)),
        "k_norm_w": gain(ks[8], (DEPTH, DA_QK_DIM)),
        "lambda_q1": nrm(ks[9], (DEPTH, DA_QK_DIM), 0.1),
        "lambda_k1": nrm(ks[10], (DEPTH, DA_QK_DIM), 0.1),
        "lambda_q2": nrm(ks[11], (DEPTH, DA_QK_DIM), 0.1),
        "lambda_k2": nrm(ks[12], (DEPTH, DA_QK_DIM), 0.1),
        "subln_w": gain(ks[13], (DEPTH, DA_VAL_DIM)),
        "w_out": nrm(ks[14], (DEPTH, MIX_WIDTH, D_MODEL), MIX_WIDTH ** -0.5),
        "norm2_w": gain(ks[15], (DEPTH, D_MODEL)),
        "router_w": nrm(ks[16], (DEPTH, D_MODEL, N_EXPERTS), D_MODEL ** -0.5),
        "w1": nrm(ks[17], (DEPTH, N_EXPERTS, D_MODEL, D_FF), D_MODEL ** -0.5),
        "w3": nrm(ks[18], (DEPTH, N_EXPERTS, D_MODEL, D_FF), D_MODEL ** -0.5),
        "w2": nrm(ks[19], (DEPTH, N_EXPERTS, D_FF, D_MODEL), D_FF ** -0.5),
    }

def reference(x_prompt, x_sample, norm1_w, w_in, hg_lb_fwd, hg_lb_bwd, hg_norm_w, q_norm_w, k_norm_w,
              lambda_q1, lambda_k1, lambda_q2, lambda_k2, subln_w, w_out, norm2_w, router_w, w1, w3, w2):
    lb_f_all = jnp.cumsum(jax.nn.softmax(hg_lb_fwd.astype(jnp.float32), axis=0), axis=0)
    lb_b_all = jnp.cumsum(jax.nn.softmax(hg_lb_bwd.astype(jnp.float32), axis=0), axis=0)
    y_prompt = x_prompt
    y_sample = x_sample
    for l in range(DEPTH):
        lp = (norm1_w[l], w_in[l],
              lb_f_all[l].reshape(HG_HEADS, HG_KEY_DIM), lb_b_all[l].reshape(HG_HEADS, HG_KEY_DIM),
              hg_norm_w[l], q_norm_w[l], k_norm_w[l],
              lambda_q1[l], lambda_k1[l], lambda_q2[l], lambda_k2[l], subln_w[l],
              w_out[l], norm2_w[l], router_w[l], w1[l], w3[l], w2[l])
        y_prompt = hybrid_layer(y_prompt, l, *lp)
        y_sample = hybrid_layer(y_sample, l, *lp)
    return (y_prompt, y_sample)


_drawn_inputs = setup_inputs


def setup_inputs(seed=0):
    import zlib

    import numpy as np

    out = dict(_drawn_inputs(seed))
    spreads = {}
    factors = {'hg_lb_fwd': 8.0,
     'hg_lb_bwd': 8.0,
     'hg_norm_w': 4.407,
     'q_norm_w': 3.783,
     'k_norm_w': 4.399,
     'lambda_q1': 5.688,
     'lambda_k1': 8.0,
     'subln_w': 3.867,
     'norm2_w': 4.108,
     'lambda_q2': 7.163,
     'lambda_k2': 8.0}
    for name, (base, spread) in spreads.items():
        noise = np.random.default_rng([zlib.crc32(name.encode()), seed]).standard_normal(out[name].shape)
        drawn = base * np.exp(spread * noise) if base else spread * noise
        out[name] = __import__('jax').numpy.asarray(drawn.astype(out[name].dtype))
    for name, factor in factors.items():
        out[name] = (out[name] * factor).astype(out[name].dtype)
    return out
```

```python
from contextlib import ExitStack

import numpy as np

import concourse.bass as bass
from concourse import mybir

F32 = mybir.dt.float32
F32R = mybir.dt.float32r
U32 = mybir.dt.uint32
U8 = mybir.dt.uint8
ALU = mybir.AluOpType
ACT = mybir.ActivationFunctionType
AX = mybir.AxisListType

P = 128
D = 1024
KT = D // P
PROMPT, SAMPLE = 256, 512
T = PROMPT + SAMPLE
TILES = T // P
PROMPT_TILES = PROMPT // P
FIRST_TILE = [0, 0, 2, 2, 2, 2]
KEY_TILES = [2, 2, 4, 4, 4, 4]
HEADS = 4
HW = HEADS * P
EPS = 1e-6
QK_DIM = 64
LAM_INIT = 0.2
HC = 256
PIECES = 8 * HW // HC
FM_PIECES = 3 * HW // HC
FM_UNITS = 3 * HEADS
TM_UNITS = (PIECES - FM_PIECES) * TILES
LEVELS = [64, 32, 16, 8, 4, 2, 1]
NL = len(LEVELS)
PER_HEAD = 1 + 2 * NL
LUS = HEADS * PER_HEAD
LAG = 3
STAGES = 4
STATE_UNITS = [(0, 0), (1, 1), (0, 2), (1, 5), (0, 3), (1, 4), (0, 4), (1, 3)]
ATT_UNITS = TILES * HEADS

EXPERTS = 16
FF = 2816
FT = FF // P
CAP_P, CAP_S = 2 * PROMPT // EXPERTS, 2 * SAMPLE // EXPERTS
SLOTS = CAP_P + CAP_S
FC = 352
NFC = FF // FC
W2_KT = [3, 3, 3, 3, 3, 3, 2, 2]
W2_AT = [sum(W2_KT[:j]) for j in range(len(W2_KT))]
CHUNKS = 2 * NFC + len(W2_KT)
RING = 6
SPLIT = 3
CHUNK = 3 * D
TILES_AFTER = [FC * (c + 1) // P for c in range(NFC)]
T_PER_EXPERT = NFC + 2


def build(nc, x, norm1, w_in, lbf, lbb, hgw, qw, kw, lams, subw, w_out, norm2, rw, w1, w3, w2,
          ident_d, masks_d, cos_d, sin_d, out, tm_d, xt_d):
    perm = ExitStack()

    def sb(stack, name, shape, dt=F32, side="left"):
        return stack.enter_context(nc.sbuf_tensor(name, shape, dt, side=side))

    def sem(name):
        return perm.enter_context(nc.semaphore(name))

    ident = sb(perm, "ident", [P, P])
    norm_w = sb(perm, "head_norm_w", [P, 2, P])
    qk_w = sb(perm, "qk_norm_w", [P, 2, QK_DIM])
    cos = sb(perm, "cos", [P, TILES, 8])
    sin = sb(perm, "sin", [P, TILES, 8])
    lam4 = sb(perm, "lambda_rows", [P, 4, QK_DIM])
    lam_p = sb(perm, "lambda_products", [P, 2, QK_DIM])
    lam_s = sb(perm, "lambda_sums", [P, 2])
    neg_lam = sb(perm, "neg_lambda", [P, 1])
    lb_raw = sb(perm, "lb_raw", [P, 2, 2, HEADS])
    lb_max = sb(perm, "lb_max", [P, 2, HEADS])
    lb = sb(perm, "lb", [P, 2, HEADS])
    one_minus_lb = sb(perm, "one_minus_lb", [P, 2, HEADS])
    stat1 = sb(perm, "stat1", [P, TILES])
    rstd1 = sb(perm, "rstd1", [P, TILES])
    qk_ss = sb(perm, "qk_ss", [P, TILES, 16])
    qk_rstd = sb(perm, "qk_rstd", [P, TILES, 16])
    head_ss = sb(perm, "head_ss", [P, TILES, 8])
    head_rstd = sb(perm, "head_rstd", [P, TILES, 8])
    stat2 = sb(perm, "stat2", [P, TILES])
    rstd2 = sb(perm, "rstd2", [P, TILES])
    neg_max = sb(perm, "neg_max", [P, ATT_UNITS, 2])
    exp_sum = sb(perm, "exp_sum", [P, ATT_UNITS, 2])
    exp_r = sb(perm, "exp_r", [P, ATT_UNITS, 2])
    chunk_decay = sb(perm, "chunk_decay", [P, 8, TILES])

    left0, right = ExitStack(), ExitStack()
    raw_w = [sb(left0, f"raw_w{i}", [P, KT, HC]) for i in range(2)]
    stage = [sb(left0, f"stage{i}", [P, HC]) for i in range(STAGES)]
    sq = [sb(left0, f"sq{i}", [P, HC]) for i in range(2)]
    first = ExitStack()
    x_in = sb(first, "x_in", [P, TILES, D])
    x_scaled = sb(first, "x_scaled", [P, TILES, D])
    norm1_bc = sb(first, "norm1_bc", [P, D])
    first.close()
    left0.close()
    mixed_stack = ExitStack()
    mixed = sb(mixed_stack, "mixed", [P, TILES, D])
    gla = ExitStack()
    gate = sb(gla, "gate", [P, 8, T])
    keys = sb(gla, "keys", [P, 8, T])
    q_fm = sb(gla, "q_fm", [P, HEADS, T])
    att_t = sb(gla, "att_t", [P, HEADS, T])
    btot = sb(gla, "btot", [P, 8, TILES])
    e2 = [sb(gla, f"e2_{i}", [P, T]) for i in range(2)]
    lev = ExitStack()
    masks = sb(lev, "masks", [P, 2 * NL, P], U8)
    restart = sb(lev, "restart", [P, T])
    lev_tmp = sb(lev, "lev_tmp", [P, T])
    mask_load = ExitStack()
    masks_f = sb(mask_load, "masks_f", [P, 2 * NL, P])
    mask_load.close()
    xl = [sb(lev, f"level{i}", [P, T]) for i in range(3)]
    lev.close()
    states = sb(gla, "states", [P, len(STATE_UNITS), HW])
    gla.close()
    xh = sb(right, "x_high", [P, KT, T], F32R, "right")
    xlo = sb(right, "x_low", [P, KT, T], F32R, "right")
    wh = [sb(right, f"w_high{i}", [P, KT, HC], F32R, "right") for i in range(2)]
    wl = [sb(right, f"w_low{i}", [P, KT, HC], F32R, "right") for i in range(2)]
    right.close()
    att = ExitStack()
    v_tm = sb(att, "v_tm", [P, TILES, HW], side="right")
    av = sb(att, "av", [P, TILES, HW], side="right")
    qt = sb(att, "q_t", [P, HEADS, T], side="right")
    kt_ = sb(att, "k_t", [P, HEADS, T], side="right")
    qk = [sb(att, f"qk{i}", [P, 2 * HW], side="right") for i in range(2)]
    rope_t = sb(att, "rope_t", [P, 4, 16, 8], side="right")
    probs = [sb(att, f"probs{i}", [P, 2, 512], side="right") for i in range(2)]
    probs_t = [sb(att, f"probs_t{i}", [P, 512], side="right") for i in range(2)]
    kdec_tm = [sb(att, f"kdec_tm{i}", [P, HW], side="right") for i in range(2)]
    sq_o = sb(att, "sq_o", [P, D], side="right")
    att.close()
    outp = ExitStack()
    woh = sb(outp, "wo_high", [P, KT, D], F32R)
    wol = sb(outp, "wo_low", [P, KT, D], F32R)
    mth = [sb(outp, f"mix_high{i}", [P, KT, P], F32R) for i in range(2)]
    mtl = [sb(outp, f"mix_low{i}", [P, KT, P], F32R) for i in range(2)]
    wo_raw = [sb(outp, f"wo_raw{i}", [P, D]) for i in range(2)]
    x_again = [sb(outp, f"x_again{i}", [P, D]) for i in range(2)]
    hg = [sb(outp, f"hg{i}", [P, HW]) for i in range(2)]
    hg_sig = [sb(outp, f"hg_sig{i}", [P, HW]) for i in range(2)]
    outp.close()
    rout = ExitStack()
    norm2_bc = sb(rout, "norm2_bc", [P, D])
    rw_sb = sb(rout, "router_w", [P, KT, EXPERTS])
    xt = [sb(rout, f"xt{i}", [P, D]) for i in range(2)]
    xtt = [sb(rout, f"xt_t{i}", [P, KT, P]) for i in range(2)]
    lmax = sb(rout, "logit_max", [P, TILES])
    logit = sb(rout, "logit", [P, TILES, EXPERTS])
    lexp = sb(rout, "logit_exp", [P, TILES, EXPERTS])
    lsum = sb(rout, "logit_sum", [P, TILES])
    aff = sb(rout, "affinity", [P, 4, 48])
    aff_t = [sb(rout, f"affinity_t{i}", [48, SAMPLE]) for i in range(2)]
    top = sb(rout, "top_values", [48, CAP_S])
    top_i = sb(rout, "top_tokens", [48, CAP_S], U32)
    slot_gate = sb(rout, "slot_gate", [48, SLOTS])
    slot_token = sb(rout, "slot_token", [48, SLOTS])
    rout.close()
    mixed_stack.close()
    moe = ExitStack()
    ring = [sb(moe, f"ring{i}", [P, CHUNK], side="right") for i in range(RING)]
    ch = [sb(moe, f"chunk_high{i}", [P, CHUNK], F32R) for i in range(SPLIT)]
    cl = [sb(moe, f"chunk_low{i}", [P, CHUNK], F32R) for i in range(SPLIT)]
    silu = [sb(moe, f"silu{i}", [SLOTS, FC]) for i in range(2)]
    hid = sb(moe, "hid", [SLOTS, FF])
    hid_h = sb(moe, "hid_high", [P, FT, SLOTS], F32R)
    hid_l = sb(moe, "hid_low", [P, FT, SLOTS], F32R)
    xe = sb(moe, "xe", [SLOTS, D])
    xeh = sb(moe, "xe_high", [P, KT, SLOTS], F32R)
    xel = sb(moe, "xe_low", [P, KT, SLOTS], F32R)
    y_sb = sb(moe, "y_rows", [SLOTS, D])
    token = sb(moe, "token", [SLOTS, EXPERTS], U32)
    gates = sb(moe, "gates", [SLOTS, EXPERTS])

    pair = [perm.enter_context(nc.psum_tensor(f"pair{i}", [P, 1024], F32)) for i in range(4)]
    PA, PB, PC, PD = pair

    consts_in = sem("consts_in")
    lb_in = sem("lb_in")
    masks_in = sem("masks_in")
    masks_done = sem("masks_done")
    norm2_in = sem("norm2_in")
    x_tile_in = [sem(f"x_tile_in{i}") for i in range(TILES)]
    w_in_sem = [sem(f"w_piece_in{i}") for i in range(2)]
    setup_v = sem("setup_v")
    setup_a = sem("setup_a")
    x_sq = sem("x_sq")
    x_std = sem("x_std")
    x_rstd = sem("x_rstd")
    xs_ready = sem("xs_ready")
    x_t = sem("x_t")
    xh_done = sem("xh_done")
    xl_done = sem("xl_done")
    wh_done = sem("w_high_done")
    wl_done = sem("w_low_done")
    fm_mm = sem("fm_mm")
    fm_act = sem("fm_act")
    q_done = sem("q_done")
    f_done = sem("f_done")
    k_done = sem("k_done")
    ln_done = sem("ln_done")
    scan_v = sem("scan_v")
    tm_mm = sem("tm_mm")
    tm_ev = sem("tm_ev")
    stage_full = sem("stage_full")
    stage_out = [sem(f"stage_out{i}") for i in range(STAGES)]
    sq_full = sem("sq_full")
    sq_used = sem("sq_used")
    x_sub = sem("level_sub")
    x_exp = sem("level_exp")
    x_rdy = sem("level_ready")
    lu_mm = sem("level_mm")
    lu_ev = sem("level_merged")
    e2_done = sem("suffix_decays_done")
    e_done = sem("decays_done")
    decay_done = sem("chunk_decay_done")
    fac = sem("factors_done")
    v_in = sem("v_in")
    av_in = sem("av_in")
    qk_in = [sem(f"qk_in{i}") for i in range(2)]
    qk_std = sem("qk_std")
    qk_v = sem("qk_v")
    qk_rdy = sem("qk_ready")
    qk_t = sem("qk_transposed")
    qk_ev = sem("qk_evacuated")
    kd_t = sem("kdec_transposed")
    kd_ev = sem("kdec_evacuated")
    u_mm = sem("update_mm")
    s_done = sem("state_done")
    sc_mm = sem("scores_mm")
    mx_v = sem("score_max_v")
    mx_done = sem("score_max")
    ex_done = sem("score_exp")
    pd_v = sem("probs_v")
    pd_rdy = sem("probs_ready")
    pt_mm = sem("probs_transposed")
    pt_ev = sem("probs_t_evacuated")
    pv_mm = sem("pv_mm")
    ao_ev = sem("attention_out")
    go_mm = sem("gla_mm")
    go_ev = sem("gla_out")
    o_sq = sem("out_squares")
    o_red = sem("out_squares_used")
    o_std = sem("out_std")
    o_v = sem("out_v")
    wo_in = [sem(f"wo_in{i}") for i in range(2)]
    woh_done = sem("wo_high_done")
    wol_done = sem("wo_low_done")
    xa_in = [sem(f"x_again_in{i}") for i in range(2)]
    hg_in = [sem(f"hg_in{i}") for i in range(2)]
    hg_act = sem("hg_sigmoid")
    mix_v = sem("mix_v")
    mix_rdy = sem("mix_ready")
    mt_mm = sem("mix_transposed")
    mth_done = sem("mix_high_done")
    mtl_done = sem("mix_low_done")
    wo_mm = sem("wo_mm")
    h_done = sem("h_done")
    h_sq = sem("h_squares")
    h_out = sem("h_out")
    h_std = sem("h_std")
    h_v = sem("h_v")
    xt_done = sem("xt_done")
    xt_out = [sem(f"xt_out{i}") for i in range(2)]
    xtt_mm = sem("xt_transposed")
    xtt_ev = sem("xt_t_evacuated")
    lg_mm = sem("logits_mm")
    rt_v = sem("router_v")
    rt_exp = sem("router_exp")
    rt_t = sem("router_transposed")
    top_v = sem("top_v")
    route_done = sem("route_done")
    raw_in = [sem(f"chunk_in{i}") for i in range(RING)]
    ch_done = sem("chunk_high_done")
    cl_done = sem("chunk_low_done")
    used = sem("chunks_used")
    silu_done = sem("silu_done")
    hid_done = sem("hid_done")
    t_mm = sem("t_mm")
    th_done = sem("t_high_done")
    tl_done = sem("t_low_done")
    xe_in = sem("xe_in")
    y_ev = sem("y_evacuated")
    y_out = sem("y_scattered")
    y_free = sem("y_rows_free")

    NCONST = 9

    def tile(t):
        return slice(t * P, (t + 1) * P)

    def level_of(i):
        h, j = divmod(i, PER_HEAD)
        return (h, None, None) if j == 0 else (h, (j - 1) // NL, (j - 1) % NL)

    def levels_to(i):
        return i + 1 - (i // PER_HEAD + 1)

    def split_slot_free(hc):
        old = hc - 2
        return (fm_mm, 2 * old + 2) if old < FM_PIECES else (tm_mm, TILES * (old - FM_PIECES + 1))

    def scores_of(a):
        return pair[a % 2]

    def chunk_view(buf, c):
        if c < 2 * NFC:
            return buf[:, 0:KT * FC].rearrange("p (k n) -> p k n", k=KT)
        k = W2_KT[c - 2 * NFC]
        return buf[:, 0:k * D].rearrange("p (k n) -> p k n", k=k)

    def chunk_size(c):
        return KT * FC if c < 2 * NFC else W2_KT[c - 2 * NFC] * D

    def load_chunk(sp, e, c, ahead=0):
        if c < 2 * NFC:
            w, c0 = (w1, w3)[c % 2], c // 2 * FC
            src = w.rearrange("e d n -> (e d) n")[bass.ds(e * D + ahead * D, D), c0:c0 + FC]
        else:
            j = c - 2 * NFC
            src = w2.rearrange("e f n -> (e f) n")[bass.ds(e * FF + (ahead * FF + W2_AT[j] * P), W2_KT[j] * P), :]
        src = src.rearrange("(k p) n -> p k n", p=P)
        sp.dma_start(chunk_view(ring[c % RING], c), src).then_inc(raw_in[c % RING], 16)

    block = perm.enter_context(nc.Block())

    @block.sync
    def _(sp):
        with nc.allow_non_contiguous_dma(reason="small constants in a transposed layout"):
            sp.dma_start(ident[:, :], ident_d).then_inc(consts_in, 16)
            for t in range(TILES):
                sp.dma_start(x_in[:, t, :], x[tile(t), :]).then_inc(x_tile_in[t], 16)
                if t == 0:
                    sp.dma_start(norm1_bc[:, :], norm1.partition_broadcast(P)).then_inc(consts_in, 16)
            for hc in range(2):
                sp.dma_start(raw_w[hc][:, :, :],
                             w_in[:, hc * HC:(hc + 1) * HC].rearrange("(k p) n -> p k n", p=P)).then_inc(w_in_sem[hc], 16)
            for i, d_lb in enumerate((lbf, lbb)):
                for r in range(2):
                    sp.dma_start(lb_raw[:, i, r, :], d_lb[r, :].rearrange("(h k) -> k h", k=P)).then_inc(lb_in, 16)
            for i, w in enumerate((hgw, subw)):
                sp.dma_start(norm_w[:, i, :], w.partition_broadcast(P)).then_inc(consts_in, 16)
            for i, w in enumerate((qw, kw)):
                sp.dma_start(qk_w[:, i, :], w.partition_broadcast(P)).then_inc(consts_in, 16)
            sp.dma_start(cos[:, :, :], cos_d).then_inc(consts_in, 16)
            sp.dma_start(sin[:, :, :], sin_d).then_inc(consts_in, 16)
            sp.dma_start(lam4[:, :, :], lams.partition_broadcast(P)).then_inc(consts_in, 16)
            sp.wait_ge(x_t, TILES)
            sp.dma_start(masks_f[:, :, :], masks_d).then_inc(masks_in, 16)
            for hc in range(PIECES):
                if hc + 2 < PIECES:
                    sp.wait_ge(wl_done, hc + 1)
                    c0 = (hc + 2) * HC
                    sp.dma_start(raw_w[hc % 2][:, :, :],
                                 w_in[:, c0:c0 + HC].rearrange("(k p) n -> p k n", p=P)).then_inc(w_in_sem[hc % 2], 16)
                if hc >= FM_PIECES:
                    for t in range(TILES):
                        n = (hc - FM_PIECES) * TILES + t
                        sp.wait_ge(stage_full, n + 1)
                        c0 = (hc - FM_PIECES) * HC
                        sp.dma_start(tm_d[tile(t), c0:c0 + HC], stage[n % STAGES][:, :]).then_inc(stage_out[n % STAGES], 16)
            sp.wait_ge(tm_mm, TM_UNITS)
            for i in range(STAGES):
                sp.wait_ge(stage_out[i], 16 * (TM_UNITS // STAGES))
            sp.dma_start(v_tm[:, :, :], tm_d[:, 0:HW].rearrange("(t p) n -> p t n", p=P)).then_inc(v_in, 16)
            for t in range(TILES):
                if t >= 2:
                    sp.wait_ge(qk_t, t - 1)
                sp.dma_start(qk[t % 2][:, :], tm_d[tile(t), 2 * HW:4 * HW]).then_inc(qk_in[t % 2], 16)
                if t == 1:
                    sp.dma_start(av[:, :, :], tm_d[:, 4 * HW:5 * HW].rearrange("(t p) n -> p t n", p=P)).then_inc(av_in, 16)
            sp.wait_ge(go_mm, TILES)
            for k in range(2):
                sp.dma_start(wo_raw[k % 2][:, :], w_out[tile(k), :]).then_inc(wo_in[k % 2], 16)
                sp.dma_start(x_again[k][:, :], x[tile(k), :]).then_inc(xa_in[k], 16)
            sp.wait_ge(o_red, TILES)
            for k in range(2):
                sp.dma_start(hg[k][:, :], tm_d[tile(k), HW:2 * HW]).then_inc(hg_in[k], 16)
            for k in range(2, KT):
                sp.wait_ge(wol_done, k - 1)
                sp.dma_start(wo_raw[k % 2][:, :], w_out[tile(k), :]).then_inc(wo_in[k % 2], 16)
            for c in range(RING):
                load_chunk(sp, 0, c)
            for t in range(TILES):
                if t + 2 < TILES:
                    sp.wait_ge(mix_rdy, t + 1)
                    sp.dma_start(hg[t % 2][:, :], tm_d[tile(t + 2), HW:2 * HW]).then_inc(hg_in[t % 2], 16)
                sp.wait_ge(h_done, t + 1)
                sp.dma_start(out[tile(t), :], mixed[:, t, :]).then_inc(h_out, 16)
                if t + 2 < TILES:
                    sp.dma_start(x_again[t % 2][:, :], x[tile(t + 2), :]).then_inc(xa_in[t % 2], 16)
            sp.wait_ge(wo_mm, TILES)
            sp.dma_start(norm2_bc[:, :], norm2.partition_broadcast(P)).then_inc(norm2_in, 16)
            sp.dma_start(rw_sb[:, :, :], rw.rearrange("(k p) e -> p k e", p=P)).then_inc(norm2_in, 16)
            for t in range(TILES):
                sp.wait_ge(xt_done, t + 1)
                sp.dma_start(xt_d[tile(t), :], xt[t % 2][:, :]).then_inc(xt_out[t % 2], 16)
            with sp.Fori(0, EXPERTS - 1) as e:
                for c in range(CHUNKS):
                    sp.wait_ge(cl_done, e * CHUNKS + (c + 1))
                    load_chunk(sp, e, (c + RING) % CHUNKS, (c + RING) // CHUNKS)
            for c in range(CHUNKS - RING):
                sp.wait_ge(cl_done, (EXPERTS - 1) * CHUNKS + c + 1)
                load_chunk(sp, EXPERTS - 1, c + RING)

    @block.tensor
    def _(pe):
        def split_mm(dst, a_high, a_low, b_high, b_low, first, last):
            pe.matmul(dst, a_high, b_high, start=first, stop=False)
            pe.matmul(dst, a_high, b_low, start=False, stop=False)
            return pe.matmul(dst, a_low, b_high, start=False, stop=last)

        pe.wait_ge(consts_in, 16 * NCONST)
        for t in range(TILES):
            pe.wait_ge(xs_ready, t + 1)
            if t >= 2:
                pe.wait_ge(xl_done, t - 1)
            for k in range(KT):
                mm = pe.transpose(pair[2 + t % 2][:, tile(k)], x_scaled[:, t, tile(k)], ident[:, :])
            mm.then_inc(x_t, 1)
        pe.wait_ge(xl_done, TILES)
        for u in range(FM_UNITS):
            hc = u // 2
            if u % 2 == 0:
                pe.wait_ge(wl_done, hc + 1)
            if u >= 2:
                if u - 2 < HEADS:
                    pe.wait_ge(q_done, u - 1)
                else:
                    pe.wait_ge(fm_act, u - 1)
            dst = pair[u % 2]
            cols = slice((u % 2) * P, (u % 2 + 1) * P)
            for k in range(KT):
                for d0, d1, x0, x1 in ((0, SAMPLE, PROMPT, T), (512, 512 + PROMPT, 0, PROMPT)):
                    mm = split_mm(dst[:, d0:d1], wh[hc % 2][:, k, cols], wl[hc % 2][:, k, cols],
                                  xh[:, k, x0:x1], xlo[:, k, x0:x1], k == 0, k == KT - 1)
            mm.then_inc(fm_mm, 1)

        def token_major(n):
            hc, t = FM_PIECES + n // TILES, n % TILES
            if t == 0:
                pe.wait_ge(wl_done, hc + 1)
            if n >= 2:
                pe.wait_ge(tm_ev, n - 1)
            dst = PC[:, (n % 2) * 512:(n % 2) * 512 + HC]
            for k in range(KT):
                mm = split_mm(dst, xh[:, k, tile(t)], xlo[:, k, tile(t)], wh[hc % 2][:, k, :],
                              wl[hc % 2][:, k, :], k == 0, k == KT - 1)
            mm.then_inc(tm_mm, 1)

        def pairs_of_level(i):
            h, d, _ = level_of(i)
            dst = pair[i % 2]
            if i < 2:
                pe.wait_ge(fm_act, FM_UNITS)
                pe.wait_ge(k_done, 8)
                pe.wait_ge(q_done, HEADS)
            else:
                pe.wait_ge(lu_ev, i - 1)
            if d is not None:
                pe.wait_ge(x_rdy, levels_to(i))
            for t in range(TILES):
                at = dst[:, t // 3 * 512 + t % 3 * P:t // 3 * 512 + t % 3 * P + P]
                if d is None:
                    pe.matmul(at, keys[:, h, tile(t)], q_fm[:, h, tile(t)], start=True, stop=False)
                    mm = pe.matmul(at, keys[:, 4 + h, tile(t)], q_fm[:, h, tile(t)], start=False, stop=True)
                else:
                    lv = xl[(levels_to(i) - 1) % 3]
                    mm = pe.matmul(at, lv[:, tile(t)], lv[:, tile(t)], start=True, stop=True)
            mm.then_inc(lu_mm, 1)

        for n in range(LUS + LAG + 1):
            if n < TM_UNITS:
                token_major(n)
            if 0 <= n - LAG - 1 < LUS:
                pairs_of_level(n - LAG - 1)

        def updates(w):
            d, t = STATE_UNITS[w]
            pe.wait_ge(kd_ev, w + 1)
            if w == 0:
                pe.wait_ge(v_in, 16)
            if w >= 2:
                pe.wait_ge(s_done, w - 1)
            for h in range(HEADS):
                mm = pe.matmul(PD[:, (w % 2) * 512 + h * P:(w % 2) * 512 + (h + 1) * P],
                               kdec_tm[w % 2][:, tile(h)], v_tm[:, t, tile(h)], start=True, stop=True)
            mm.then_inc(u_mm, 1)

        pe.wait_ge(lu_ev, LUS)
        pe.wait_ge(tm_ev, TM_UNITS)
        for w in range(len(STATE_UNITS) + 1):
            if w < len(STATE_UNITS):
                d, t = STATE_UNITS[w]
                if w == 0:
                    pe.wait_ge(fac, 16)
                if w >= 2:
                    pe.wait_ge(kd_ev, w - 1)
                for h in range(HEADS):
                    mm = pe.transpose(PC[:, (w % 2) * 512 + h * P:(w % 2) * 512 + (h + 1) * P],
                                      keys[:, d * 4 + h, tile(t)], ident[:, :])
                mm.then_inc(kd_t, 1)
            if w < TILES:
                pe.wait_ge(qk_rdy, w + 1)
                if w >= 2:
                    pe.wait_ge(qk_ev, w - 1)
                for j in range(2 * HEADS):
                    mm = pe.transpose(pair[w % 2][:, tile(j)], qk[w % 2][:, tile(j)], ident[:, :])
                mm.then_inc(qk_t, 1)
            if w >= 1:
                updates(w - 1)

        def scores(a):
            t, h = divmod(a, HEADS)
            n = KEY_TILES[t] * P
            k0 = FIRST_TILE[t] * P
            if a < 2:
                pe.wait_ge(qk_ev, TILES)
            else:
                pe.wait_ge(ex_done, a - 1)
            for c in range(2):
                rows = slice(c * QK_DIM, (c + 1) * QK_DIM)
                mm = pe.matmul(scores_of(a)[:, c * 512:c * 512 + n], qt[rows, h, tile(t)],
                               kt_[rows, h, k0:k0 + n], start=True, stop=True)
            mm.then_inc(sc_mm, 1)

        def transpose_probs(a):
            t, h = divmod(a, HEADS)
            pe.wait_ge(pd_rdy, a + 1)
            if a < 2:
                pe.wait_ge(kd_ev, len(STATE_UNITS))
            else:
                pe.wait_ge(pt_ev, a - 1)
            for k in range(KEY_TILES[t]):
                mm = pe.transpose(PC[:, (a % 2) * 512 + k * P:(a % 2) * 512 + (k + 1) * P],
                                  probs[a % 2][:, 0, tile(k)], ident[:, :])
            mm.then_inc(pt_mm, 1)

        def values(a):
            t, h = divmod(a, HEADS)
            pe.wait_ge(pt_ev, a + 1)
            if a == 0:
                pe.wait_ge(av_in, 16)
                pe.wait_ge(s_done, len(STATE_UNITS))
            if h == 0 and t >= 1:
                pe.wait_ge(ao_ev, t)
            for k in range(KEY_TILES[t]):
                mm = pe.matmul(PD[:, tile(h)], probs_t[a % 2][:, tile(k)],
                               av[:, FIRST_TILE[t] + k, tile(h)], start=k == 0, stop=k == KEY_TILES[t] - 1)
            mm.then_inc(pv_mm, 1)

        def hgrn_out(t):
            if t >= 1:
                pe.wait_ge(go_ev, t)
            else:
                pe.wait_ge(s_done, len(STATE_UNITS))
                pe.wait_ge(lu_ev, LUS)
            for h in range(HEADS):
                dst = PD[:, 512 + h * P:512 + (h + 1) * P]
                terms = [(att_t[:, h, tile(t)], v_tm[:, t, tile(h)])]
                if (0, t - 1) in STATE_UNITS:
                    terms.append((gate[:, h, tile(t)], states[:, STATE_UNITS.index((0, t - 1)), tile(h)]))
                if (1, t + 1) in STATE_UNITS:
                    terms.append((gate[:, 4 + h, tile(t)], states[:, STATE_UNITS.index((1, t + 1)), tile(h)]))
                for i, (a, b) in enumerate(terms):
                    mm = pe.matmul(dst, a, b, start=i == 0, stop=i == len(terms) - 1)
            mm.then_inc(go_mm, 1)

        for a in range(ATT_UNITS + 2):
            if a < ATT_UNITS:
                scores(a)
            if 1 <= a <= ATT_UNITS:
                transpose_probs(a - 1)
            if a % HEADS == HEADS - 1 and a // HEADS < TILES:
                hgrn_out(a // HEADS)
            if a >= 2:
                values(a - 2)

        def transpose_mix(t):
            pe.wait_ge(mix_rdy, t + 1)
            if t == 0:
                pe.wait_ge(ao_ev, TILES)
                pe.wait_ge(go_ev, TILES)
            if t >= 2:
                pe.wait_ge(mtl_done, t - 1)
            for k in range(KT):
                mm = pe.transpose(pair[2 + t % 2][:, tile(k)], mixed[:, t, tile(k)], ident[:, :])
            mm.then_inc(mt_mm, 1)

        transpose_mix(0)
        for t in range(TILES):
            if t + 1 < TILES:
                transpose_mix(t + 1)
            pe.wait_ge(mtl_done, t + 1)
            if t == 0:
                pe.wait_ge(ex_done, ATT_UNITS)
            if t >= 2:
                pe.wait_ge(h_sq, t - 1)
            for k in range(KT):
                if t == 0:
                    pe.wait_ge(wol_done, k + 1)
                for half in range(2):
                    cols = slice(half * 512, (half + 1) * 512)
                    mm = split_mm(pair[t % 2][:, cols], mth[t % 2][:, k, :], mtl[t % 2][:, k, :],
                                  woh[:, k, cols], wol[:, k, cols], k == 0, k == KT - 1)
            mm.then_inc(wo_mm, 1)

        pe.wait_ge(norm2_in, 32)
        pe.wait_ge(h_sq, TILES)
        for t in range(TILES + 1):
            if t < TILES:
                pe.wait_ge(xt_done, t + 1)
                if t >= 2:
                    pe.wait_ge(xtt_ev, t - 1)
                for k in range(KT):
                    mm = pe.transpose(pair[2 + t % 2][:, tile(k)], xt[t % 2][:, tile(k)], ident[:, :])
                mm.then_inc(xtt_mm, 1)
            if t >= 1:
                pe.wait_ge(xtt_ev, t)
                for k in range(KT):
                    mm = pe.matmul(PA[:, (t - 1) * EXPERTS:t * EXPERTS], xtt[(t - 1) % 2][:, k, :],
                                   rw_sb[:, k, :], start=k == 0, stop=k == KT - 1)
                mm.then_inc(lg_mm, 1)
        pe.wait_ge(rt_v, 8)
        for j in range(4):
            mm = pe.transpose(PB[0:48, tile(j)], aff[:, j, :], ident[:, :])
        mm.then_inc(rt_t, 1)
        pe.wait_ge(top_v, 3 * (CAP_S // 8) + 7)
        pe.transpose(PC[0:SLOTS, 0:48], slot_token[:, :], ident[0:48, 0:48])
        pe.transpose(PC[0:SLOTS, 64:112], slot_gate[:, :], ident[0:48, 0:48]).then_inc(rt_t, 1)

        H1, H3 = (PA[:, 0:512], PA[:, 512:1024]), (PB[:, 0:512], PB[:, 512:1024])
        TB = (PC[:, 0:512], PC[:, 512:1024])

        def transpose_rows(j, value):
            if j == 0:
                pe.wait_ge(xe_in, value)
            for k in range(4):
                mm = pe.transpose(TB[j][:, k * SLOTS:(k + 1) * SLOTS], xe[:, tile(4 * j + k)],
                                  ident[0:SLOTS, 0:SLOTS])
            mm.then_inc(t_mm, 1)

        pe.wait_ge(route_done, 2)
        for j in range(2):
            transpose_rows(j, 16)
        pe.sem_inc(used, SPLIT)

        def expert(e, last):
            def hid_tiles(fc):
                return range(TILES_AFTER[fc - 1] if fc else 0, TILES_AFTER[fc])

            for c in range(CHUNKS):
                pe.wait_ge(cl_done, e * CHUNKS + (c + 1))
                hi, lo = chunk_view(ch[c % SPLIT], c), chunk_view(cl[c % SPLIT], c)
                if c < 2 * NFC:
                    fc = c // 2
                    if c == 0:
                        pe.wait_ge(tl_done, e * T_PER_EXPERT + 2)
                    if c % 2 == 0:
                        pe.wait_ge(hid_done, e * NFC + (fc + 1))
                    dst = (H1, H3)[c % 2][fc % 2][0:SLOTS, 0:FC]
                    for k in range(KT):
                        mm = split_mm(dst, xeh[:, k, :], xel[:, k, :], hi[:, k, :], lo[:, k, :],
                                      k == 0, k == KT - 1)
                else:
                    j = c - 2 * NFC
                    if j == 0:
                        pe.wait_ge(y_ev, e + 1)
                    if j == len(W2_KT) - 2:
                        pe.wait_ge(tl_done, e * T_PER_EXPERT + (2 + NFC))
                    elif j == 0:
                        pe.wait_ge(tl_done, e * T_PER_EXPERT + (1 + NFC))
                    for k in range(W2_KT[j]):
                        kk = W2_AT[j] + k
                        for half in range(2):
                            cols = slice(half * 512, (half + 1) * 512)
                            mm = split_mm(PD[0:SLOTS, cols], hid_h[:, kk, :], hid_l[:, kk, :],
                                          hi[:, k, cols], lo[:, k, cols], kk == 0, kk == FT - 1)
                mm.then_inc(used, 1)
                if c >= 2 and c % 2 == 0 and c // 2 - 1 < NFC:
                    fc = c // 2 - 1
                    pe.wait_ge(hid_done, e * NFC + (fc + 3))
                    pe.wait_ge(tl_done, e * T_PER_EXPERT + (1 + fc))
                    for i, k in enumerate(hid_tiles(fc)):
                        mm = pe.transpose(TB[fc % 2][:, i * SLOTS:(i + 1) * SLOTS], hid[:, tile(k)],
                                          ident[0:SLOTS, 0:SLOTS])
                    mm.then_inc(t_mm, 1)
                if not last and c in (2 * NFC + 2, 2 * NFC + 3):
                    j = c - 2 * NFC - 2
                    pe.wait_ge(tl_done, e * T_PER_EXPERT + (1 + NFC + j))
                    transpose_rows(j, e * 16 + 32)

        with pe.Fori(0, EXPERTS - 1) as e:
            expert(e, False)
        expert(EXPERTS - 1, True)

    @block.scalar
    def _(act):
        def high_part(hc):
            act.wait_ge(w_in_sem[hc % 2], 16 * (hc // 2 + 1))
            if hc >= 2:
                act.wait_ge(*split_slot_free(hc))
            act.activation(wh[hc % 2][:, :, :], raw_w[hc % 2][:, :, :], ACT.Copy).then_inc(wh_done, 1)

        for t in range(TILES):
            act.wait_ge(x_tile_in[t], 16)
            if t >= 2:
                act.wait_ge(x_sq, t - 1)
            act.activation(pair[t % 2][:, :], x_in[:, t, :], ACT.Square, accum_out=stat1[:, t:t + 1]).then_inc(x_sq, 1)
        act.wait_ge(setup_v, 1)
        act.activation(rstd1[:, :], stat1[:, :], ACT.Sqrt).then_inc(x_std, 1)
        high_part(0)
        for t in range(TILES):
            act.wait_ge(x_t, t + 1)
            act.activation(xh[:, :, tile(t)], pair[2 + t % 2][:, :].rearrange("p (k n) -> p k n", k=KT),
                           ACT.Copy).then_inc(xh_done, 1)
        high_part(1)
        act.wait_ge(setup_v, 6)
        act.activation(lam_s[:, :], lam_s[:, :], ACT.Exp).then_inc(setup_a, 1)
        act.activation(lb_raw[:, :, :, :], lb_raw[:, :, :, :], ACT.Exp).then_inc(setup_a, 1)
        for u in range(FM_UNITS):
            if u % 2 == 0 and u >= 2:
                high_part(u // 2 + 1)
            act.wait_ge(fm_mm, u + 1)
            if u < HEADS:
                if u >= 2:
                    act.wait_ge(q_done, u - 1)
                dst = e2[u % 2][:, :]
            else:
                dst = gate[:, u - HEADS, :]
            if u == 0:
                act.wait_ge(x_t, TILES)
            act.activation(dst[:, PROMPT:T], pair[u % 2][:, 0:SAMPLE], ACT.Sigmoid)
            act.activation(dst[:, 0:PROMPT], pair[u % 2][:, 512:512 + PROMPT], ACT.Sigmoid).then_inc(fm_act, 1)
        high_part(FM_PIECES + 1)
        for hd in range(8):
            act.wait_ge(k_done, hd + 1)
            act.activation(gate[:, hd, :], gate[:, hd, :], ACT.Ln).then_inc(ln_done, 1)

        def evacuate_projection(n):
            act.wait_ge(tm_mm, n + 1)
            if n >= STAGES:
                act.wait_ge(stage_out[n % STAGES], 16 * (n // STAGES))
            src = PC[:, (n % 2) * 512:(n % 2) * 512 + HC]
            piece = n // TILES
            normed = 4 <= piece < 8
            ins = act.activation(stage[n % STAGES][:, :], src, ACT.Copy).then_inc(stage_full, 1)
            if normed:
                m = n - 4 * TILES
                if m >= 2:
                    act.wait_ge(sq_used, m - 1)
                act.activation(sq[m % 2][:, :], src, ACT.Square).then_inc(sq_full, 1)
                act.wait_ge(sq_full, m + 1)
            act.wait_ge(stage_full, n + 1)
            act.sem_inc(tm_ev, 1)

        def decays(h):
            for d in range(2):
                hd = d * 4 + h
                if h >= 1:
                    act.wait_ge(fac, 4 * h)
                for t in range(TILES):
                    act.activation(e2[d][:, tile(t)], gate[:, hd, tile(t)], ACT.Exp,
                                   bias=btot[:, hd, t:t + 1], scale=-1.0).then_inc(e2_done, 1)
                act.wait_ge(e2_done, TILES * (2 * h + d + 1))
                act.activation(gate[:, hd, :], gate[:, hd, :], ACT.Exp).then_inc(e_done, 1)

        for n in range(LUS + LAG + 1):
            i = n - LAG
            if n >= TILES and n % TILES == 0 and FM_PIECES + 1 + n // TILES < PIECES:
                high_part(FM_PIECES + 1 + n // TILES)
            if n < TM_UNITS:
                evacuate_projection(n)
            if i == 0:
                act.wait_ge(scan_v, 24)
                act.activation(chunk_decay[:, :, :], btot[:, :, :], ACT.Exp).then_inc(decay_done, 1)
            if i >= PER_HEAD and i % PER_HEAD == 0:
                decays(i // PER_HEAD - 1)
            if 0 <= i < LUS and level_of(i)[1] is not None:
                lv = levels_to(i)
                act.wait_ge(x_sub, lv)
                act.activation(xl[(lv - 1) % 3][:, :], xl[(lv - 1) % 3][:, :], ACT.Exp).then_inc(x_exp, 1)
        act.wait_ge(qk_v, 1)
        act.activation(qk_rstd[:, :, :], qk_ss[:, :, :], ACT.Sqrt).then_inc(qk_std, 1)
        for w in range(len(STATE_UNITS)):
            act.wait_ge(kd_t, w + 1)
            if w >= 2:
                act.wait_ge(u_mm, w - 1)
            act.activation(kdec_tm[w % 2][:, :], PC[:, (w % 2) * 512:(w % 2 + 1) * 512], ACT.Copy).then_inc(kd_ev, 1)
            if w < TILES:
                act.wait_ge(qk_t, w + 1)
                act.activation(qt[:, :, tile(w)], pair[w % 2][:, 0:512].rearrange("p (h n) -> p h n", h=HEADS), ACT.Copy)
                act.activation(kt_[:, :, tile(w)], pair[w % 2][:, 512:1024].rearrange("p (h n) -> p h n", h=HEADS),
                               ACT.Copy).then_inc(qk_ev, 1)

        def evac_probs(a):
            n = KEY_TILES[a // HEADS] * P
            act.wait_ge(pt_mm, a + 1)
            if a >= 2:
                act.wait_ge(pv_mm, a - 1)
            act.activation(probs_t[a % 2][:, 0:n], PC[:, (a % 2) * 512:(a % 2) * 512 + n], ACT.Copy).then_inc(pt_ev, 1)

        for a in range(ATT_UNITS + 3):
            if a < ATT_UNITS:
                n = KEY_TILES[a // HEADS] * P
                act.wait_ge(mx_done, a + 1)
                if a >= 2:
                    act.wait_ge(pt_mm, a - 1)
                for c in range(2):
                    ins = act.activation(probs[a % 2][:, c, 0:n], scores_of(a)[:, c * 512:c * 512 + n], ACT.Exp,
                                         bias=neg_max[:, a, c:c + 1], scale=QK_DIM ** -0.5,
                                         accum_out=exp_sum[:, a, c:c + 1])
                ins.then_inc(ex_done, 1)
            if 1 <= a <= ATT_UNITS:
                evac_probs(a - 1)
            if a >= HEADS + 2 and (a - 2) % HEADS == 0:
                t = (a - 2) // HEADS - 1
                act.wait_ge(pv_mm, HEADS * (t + 1))
                act.wait_ge(go_mm, t + 1)
                act.activation(mixed[:, t, 512:1024], PD[:, 0:512], ACT.Copy).then_inc(ao_ev, 1)
                act.activation(mixed[:, t, 0:512], PD[:, 512:1024], ACT.Copy).then_inc(go_ev, 1)
                if t >= 1:
                    act.wait_ge(o_red, t)
                act.wait_ge(ao_ev, t + 1)
                act.wait_ge(go_ev, t + 1)
                act.activation(sq_o[:, :], mixed[:, t, :], ACT.Square).then_inc(o_sq, 1)
        act.wait_ge(o_v, 1)
        act.activation(head_rstd[:, :, :], head_ss[:, :, :], ACT.Sqrt).then_inc(o_std, 1)

        def mix_high(t):
            act.wait_ge(mt_mm, t + 1)
            if t >= 2:
                act.wait_ge(wo_mm, t - 1)
            act.activation(mth[t % 2][:, :, :], pair[2 + t % 2][:, :].rearrange("p (k n) -> p k n", k=KT),
                           ACT.Copy).then_inc(mth_done, 1)

        def gate_sigmoid(t):
            act.wait_ge(hg_in[t % 2], 16 * (t // 2 + 1))
            if t >= 2:
                act.wait_ge(mix_rdy, t - 1)
            act.activation(hg_sig[t % 2][:, :], hg[t % 2][:, :], ACT.Sigmoid).then_inc(hg_act, 1)

        act.wait_ge(go_mm, TILES)
        gate_sigmoid(0)
        gate_sigmoid(1)
        for k in range(KT):
            act.wait_ge(wo_in[k % 2], 16 * (k // 2 + 1))
            act.activation(woh[:, k, :], wo_raw[k % 2][:, :], ACT.Copy).then_inc(woh_done, 1)
            if k == 5:
                mix_high(0)
        for t in range(TILES):
            if t + 1 < TILES:
                mix_high(t + 1)
            if t + 2 < TILES:
                gate_sigmoid(t + 2)
            act.wait_ge(h_done, t + 1)
            act.activation(pair[t % 2][:, :], mixed[:, t, :], ACT.Square, accum_out=stat2[:, t:t + 1]).then_inc(h_sq, 1)
        act.wait_ge(h_v, 1)
        act.activation(rstd2[:, :], stat2[:, :], ACT.Sqrt).then_inc(h_std, 1)
        for t in range(TILES):
            act.wait_ge(xtt_mm, t + 1)
            if t >= 2:
                act.wait_ge(lg_mm, t - 1)
            act.activation(xtt[t % 2][:, :, :], pair[2 + t % 2][:, :].rearrange("p (k n) -> p k n", k=KT),
                           ACT.Copy).then_inc(xtt_ev, 1)
        act.wait_ge(rt_v, 3)
        act.activation(lexp[:, :, :], logit[:, :, :], ACT.Exp).then_inc(rt_exp, 1)

        H1 = (PA[:, 0:512], PA[:, 512:1024])
        TB = (PC[:, 0:512], PC[:, 512:1024])

        def rows_high(j, value):
            act.wait_ge(t_mm, value)
            act.activation(xeh[:, 4 * j:4 * j + 4, :], TB[j][:, 0:4 * SLOTS].rearrange("p (k n) -> p k n", k=4),
                           ACT.Copy).then_inc(th_done, 1)

        def chunk_high(e, c):
            act.wait_ge(raw_in[c % RING], e * (16 * CHUNKS // RING) + 16 * (c // RING + 1))
            act.wait_ge(used, e * CHUNKS + (c + 1))
            n = chunk_size(c % CHUNKS)
            act.activation(ch[c % SPLIT][:, 0:n], ring[c % RING][:, 0:n], ACT.Copy).then_inc(ch_done, 1)

        def expert(e, last):
            for cc in range(2, CHUNKS + 2):
                if cc < CHUNKS or not last:
                    chunk_high(e, cc)
                c = cc - 2
                if c % 2 == 0 and c < 2 * NFC:
                    fc = c // 2
                    act.wait_ge(used, e * CHUNKS + (c + 1 + SPLIT))
                    act.activation(silu[fc % 2][:, :], H1[fc % 2][0:SLOTS, 0:FC], ACT.Silu).then_inc(silu_done, 1)
                if c >= 2 and c % 2 == 0 and c // 2 - 1 < NFC:
                    fc = c // 2 - 1
                    k0, k1 = (TILES_AFTER[fc - 1] if fc else 0), TILES_AFTER[fc]
                    act.wait_ge(t_mm, e * T_PER_EXPERT + (3 + fc))
                    act.activation(hid_h[:, k0:k1, :],
                                   TB[fc % 2][:, 0:(k1 - k0) * SLOTS].rearrange("p (k n) -> p k n", k=k1 - k0),
                                   ACT.Copy).then_inc(th_done, 1)
                if not last and c in (2 * NFC + 2, 2 * NFC + 3):
                    j = c - 2 * NFC - 2
                    rows_high(j, e * T_PER_EXPERT + (3 + NFC + j))
                if c == CHUNKS - 1:
                    act.wait_ge(used, e * CHUNKS + (CHUNKS + SPLIT))
                    act.wait_ge(y_free, e + 1)
                    for half in range(2):
                        cols = slice(half * 512, (half + 1) * 512)
                        ins = act.activation(y_sb[:, cols], PD[0:SLOTS, cols], ACT.Copy, scale=gates[:, bass.ds(e, 1)])
                    ins.then_inc(y_ev, 1)

        act.wait_ge(route_done, 2)
        rows_high(0, 1)
        rows_high(1, 2)
        chunk_high(0, 0)
        chunk_high(0, 1)
        act.sem_inc(y_ev, 1)
        with act.Fori(0, EXPERTS - 1) as e:
            expert(e, False)
        expert(EXPERTS - 1, True)

    @block.vector
    def _(dve):
        def low_part(hc):
            dve.wait_ge(wh_done, hc + 1)
            dve.tensor_tensor(wl[hc % 2][:, :, :], raw_w[hc % 2][:, :, :], wh[hc % 2][:, :, :].bitcast(F32),
                              ALU.subtract).then_inc(wl_done, 1)

        dve.wait_ge(x_sq, TILES)
        dve.tensor_scalar(stat1[:, :], stat1[:, :], 1.0 / D, EPS, ALU.mult, ALU.add).then_inc(setup_v, 1)
        dve.wait_ge(x_std, 1)
        dve.reciprocal(rstd1[:, :], rstd1[:, :]).then_inc(x_rstd, 1)
        dve.wait_ge(x_rstd, 1)
        dve.wait_ge(consts_in, 16 * NCONST)
        for t in range(TILES):
            dve.scalar_tensor_tensor(out=x_scaled[:, t, :], in0=x_in[:, t, :], scalar=rstd1[:, t:t + 1],
                                     in1=norm1_bc[:, :], op0=ALU.mult, op1=ALU.mult).then_inc(xs_ready, 1)
        low_part(0)
        for i in range(2):
            dve.tensor_tensor(lam_p[:, i, :], lam4[:, 2 * i, :], lam4[:, 2 * i + 1, :], ALU.mult).then_inc(setup_v, 1)
        dve.wait_ge(lb_in, 64)
        dve.tensor_tensor(lb_max[:, :, :], lb_raw[:, :, 0, :], lb_raw[:, :, 1, :], ALU.max).then_inc(setup_v, 1)
        dve.wait_ge(setup_v, 4)
        dve.tensor_reduce(lam_s[:, :], lam_p[:, :, :], AX.X, ALU.add).then_inc(setup_v, 1)
        for r in range(2):
            ins = dve.tensor_tensor(lb_raw[:, :, r, :], lb_raw[:, :, r, :], lb_max[:, :, :], ALU.subtract)
        ins.then_inc(setup_v, 1)
        for t in range(TILES):
            dve.wait_ge(xh_done, t + 1)
            dve.tensor_tensor(xlo[:, :, tile(t)], pair[2 + t % 2][:, :].rearrange("p (k n) -> p k n", k=KT),
                              xh[:, :, tile(t)].bitcast(F32), ALU.subtract).then_inc(xl_done, 1)
        low_part(1)
        dve.wait_ge(setup_a, 2)
        dve.tensor_tensor(neg_lam[:, :], lam_s[:, 1:2], lam_s[:, 0:1], ALU.subtract).then_inc(setup_v, 1)
        dve.tensor_tensor(lb_max[:, :, :], lb_raw[:, :, 0, :], lb_raw[:, :, 1, :], ALU.add).then_inc(setup_v, 1)
        dve.wait_ge(setup_v, 8)
        dve.tensor_scalar(neg_lam[:, :], neg_lam[:, :], -LAM_INIT, None, ALU.add).then_inc(setup_v, 1)
        dve.reciprocal(lb_max[:, :, :], lb_max[:, :, :]).then_inc(setup_v, 1)
        dve.tensor_scalar(norm_w[:, 1, :], norm_w[:, 1, :], 1.0 - LAM_INIT, None, ALU.mult).then_inc(setup_v, 1)
        dve.wait_ge(setup_v, 11)
        dve.tensor_tensor(lb[:, :, :], lb_raw[:, :, 0, :], lb_max[:, :, :], ALU.mult).then_inc(setup_v, 1)
        dve.wait_ge(setup_v, 12)
        dve.tensor_scalar(one_minus_lb[:, :, :], lb[:, :, :], -1.0, 1.0, ALU.mult, ALU.add).then_inc(setup_v, 1)
        dve.wait_ge(setup_v, 13)
        dve.wait_ge(x_t, TILES)
        for u in range(FM_UNITS):
            if u % 2 == 0 and u >= 2:
                low_part(u // 2 + 1)
            dve.wait_ge(fm_act, u + 1)
            if u < HEADS:
                for d0, d1, p0 in ((PROMPT, T, 0), (0, PROMPT, 512)):
                    ins = dve.scalar_tensor_tensor(out=q_fm[:, u, d0:d1], in0=pair[u % 2][:, p0:p0 + d1 - d0],
                                                   scalar=float(P) ** -0.5, in1=e2[u % 2][:, d0:d1],
                                                   op0=ALU.mult, op1=ALU.mult)
                ins.then_inc(q_done, 1)
            else:
                hd = u - HEADS
                d, h = divmod(hd, HEADS)
                dve.tensor_scalar(gate[:, hd, :], gate[:, hd, :], one_minus_lb[:, d, h:h + 1], lb[:, d, h:h + 1],
                                  ALU.mult, ALU.add).then_inc(f_done, 1)
                dve.wait_ge(f_done, hd + 1)
                dve.tensor_scalar(keys[:, hd, :], gate[:, hd, :], -1.0, 1.0, ALU.mult, ALU.add).then_inc(k_done, 1)
        low_part(FM_PIECES + 1)
        dve.memset(restart[:, :], 1.0).then_inc(scan_v, 1)
        dve.wait_ge(scan_v, 1)
        starts = restart[:, :].rearrange("p (t n) -> p t n", n=P)
        dve.memset(starts[:, :, 0:1], 0.0).then_inc(scan_v, 1)
        dve.wait_ge(scan_v, 2)
        done = 2
        for hd in range(8):
            dve.wait_ge(ln_done, hd + 1)
            dst = gate[:, hd, :] if hd < 4 else lev_tmp[:, :]
            if hd > 4:
                dve.wait_ge(scan_v, done)
            dve.tensor_tensor_scan(dst, restart[:, :], gate[:, hd, :], 0.0, ALU.mult, ALU.add).then_inc(scan_v, 1)
            done += 1
            dve.wait_ge(scan_v, done)
            ends = dst.rearrange("p (t n) -> p t n", n=P)
            dve.tensor_copy(btot[:, hd, :].unsqueeze(2), ends[:, :, P - 1:P]).then_inc(scan_v, 1)
            done += 1
            if hd >= 4:
                dve.tensor_tensor(gate[:, hd, :], lev_tmp[:, :], gate[:, hd, :], ALU.subtract).then_inc(scan_v, 1)
                done += 1
        done += 2
        assert done == 24, done
        dve.sem_inc(scan_v, 2)
        dve.wait_ge(scan_v, done)

        def level_views(i):
            h, d, l = level_of(i)
            m = LEVELS[l]
            buf = xl[(levels_to(i) - 1) % 3][:, :].rearrange("p (b s m) -> p b s m", s=2, m=m)

            def halves(a):
                v = a.rearrange("p (b s m) -> p b s m", s=2, m=m)
                return v[:, :, 0, :], v[:, :, 1, :]

            b0, b1 = halves(gate[:, d * 4 + h, :])
            mid = b0[:, :, m - 1:m] if d == 0 else b1[:, :, 0:1]
            return h, d, m, buf[:, :, 0, :], buf[:, :, 1, :], b0, b1, mid.to_broadcast([P, T // (2 * m), m]), halves

        def subtract(i):
            if level_of(i)[1] is None:
                return
            h, d, m, x0, x1, b0, b1, mid, _ = level_views(i)
            if levels_to(i) > 3:
                last = next(j for j in range(i) if levels_to(j) == levels_to(i) - 3 and level_of(j)[1] is not None)
                dve.wait_ge(lu_mm, last + 1)
            dve.tensor_tensor(x0, mid, b0, ALU.subtract)
            dve.tensor_tensor(x1, b1, mid, ALU.subtract).then_inc(x_sub, 1)

        def multiply(i):
            if level_of(i)[1] is None:
                return
            h, d, m, x0, x1, b0, b1, mid, halves = level_views(i)
            k0, k1 = halves(keys[:, d * 4 + h, :])
            q0, q1 = halves(q_fm[:, h, :])
            dve.wait_ge(x_exp, levels_to(i))
            dve.tensor_tensor(x0, x0, k0 if d == 0 else q0, ALU.mult)
            dve.tensor_tensor(x1, x1, q1 if d == 0 else k1, ALU.mult).then_inc(x_rdy, 1)

        def merge(i):
            h, d, l = level_of(i)
            dve.wait_ge(lu_mm, i + 1)
            if d is not None:
                dve.wait_ge(lu_ev, i)
            for g in range(2):
                dst = att_t[:, h, g * 384:(g + 1) * 384].rearrange("p (t n) -> p t n", n=P)
                src = pair[i % 2][:, g * 512:g * 512 + 384].rearrange("p (t n) -> p t n", n=P)
                if d is None:
                    ins = dve.tensor_tensor(dst, src, ident[:, :].unsqueeze(1).to_broadcast([P, 3, P]), ALU.mult)
                else:
                    mask = masks[:, d * NL + l, :].unsqueeze(1).to_broadcast([P, 3, P])
                    ins = dve.copy_predicated(dst, mask, src)
            ins.then_inc(lu_ev, 1)

        def projection_squares(n):
            m = n - 4 * TILES
            piece, t = divmod(m, TILES)
            dve.wait_ge(sq_full, m + 1)
            dve.tensor_reduce(qk_ss[:, t, piece * 4:piece * 4 + 4],
                              sq[m % 2][:, :].rearrange("p (g n) -> p g n", n=QK_DIM), AX.X, ALU.add).then_inc(sq_used, 1)

        dve.wait_ge(masks_in, 16)
        dve.tensor_copy(masks[:, :, :], masks_f[:, :, :]).then_inc(masks_done, 1)
        dve.wait_ge(masks_done, 1)
        for n in range(LUS + LAG + 2):
            i = n - LAG
            if n >= TILES and n % TILES == 0 and FM_PIECES + 1 + n // TILES < PIECES:
                low_part(FM_PIECES + 1 + n // TILES)
            if 0 <= i < LUS:
                subtract(i)
            if 0 <= i - 1 < LUS:
                multiply(i - 1)
            if 0 <= i - 2 < LUS:
                merge(i - 2)
            if 4 * TILES <= n - 1 < 8 * TILES:
                projection_squares(n - 1)
        dve.wait_ge(sq_used, 4 * TILES)
        dve.tensor_scalar(qk_ss[:, :, :], qk_ss[:, :, :], 1.0 / QK_DIM, EPS, ALU.mult, ALU.add).then_inc(qk_v, 1)
        dve.wait_ge(qk_std, 1)
        dve.reciprocal(qk_rstd[:, :, :], qk_rstd[:, :, :]).then_inc(qk_v, 1)

        def state(w):
            d, t = STATE_UNITS[w]
            before = (d, t - 1 if d == 0 else t + 1)
            dve.wait_ge(u_mm, w + 1)
            src = PD[:, (w % 2) * 512:(w % 2 + 1) * 512]
            if before not in STATE_UNITS:
                dve.tensor_copy(states[:, w, :], src).then_inc(s_done, 1)
                return
            old = STATE_UNITS.index(before)
            dve.wait_ge(s_done, old + 1)
            dve.wait_ge(decay_done, 1)
            for h in range(HEADS):
                ins = dve.scalar_tensor_tensor(out=states[:, w, tile(h)], in0=states[:, old, tile(h)],
                                               scalar=chunk_decay[:, d * 4 + h, t:t + 1], in1=src[:, tile(h)],
                                               op0=ALU.mult, op1=ALU.add)
            ins.then_inc(s_done, 1)

        qv = 2
        for w in range(len(STATE_UNITS) + 1):
            if w < TILES:
                t = w
                dve.wait_ge(qk_v, qv)
                dve.wait_ge(qk_in[t % 2], 16 * (t // 2 + 1))
                g = qk[t % 2][:, :].rearrange("p (g n) -> p g n", n=QK_DIM)
                dve.tensor_tensor(g, g, qk_rstd[:, t, :].unsqueeze(2).to_broadcast([P, 16, QK_DIM]), ALU.mult).then_inc(qk_v, 1)
                dve.wait_ge(qk_v, qv + 1)
                g4 = qk[t % 2][:, :].rearrange("p (s g n) -> p s g n", s=2, n=QK_DIM)
                dve.tensor_tensor(g4, g4, qk_w[:, :, :].unsqueeze(2).to_broadcast([P, 2, 8, QK_DIM]), ALU.mult).then_inc(qk_v, 1)
                dve.wait_ge(qk_v, qv + 2)
                x1, x2 = g[:, :, 0:8], g[:, :, 8:16]
                c_b = cos[:, t, :].unsqueeze(1).to_broadcast([P, 16, 8])
                s_b = sin[:, t, :].unsqueeze(1).to_broadcast([P, 16, 8])
                for r, (a, b) in enumerate(((x1, c_b), (x2, s_b), (x2, c_b), (x1, s_b))):
                    ins = dve.tensor_tensor(rope_t[:, r, :, :], a, b, ALU.mult)
                ins.then_inc(qk_v, 1)
                dve.wait_ge(qk_v, qv + 3)
                dve.tensor_tensor(x1, rope_t[:, 0, :, :], rope_t[:, 1, :, :], ALU.subtract)
                dve.tensor_tensor(x2, rope_t[:, 2, :, :], rope_t[:, 3, :, :], ALU.add).then_inc(qk_rdy, 1)
                qv += 3
            if w >= 1:
                state(w - 1)

        def score_max(a):
            n = KEY_TILES[a // HEADS] * P
            dve.wait_ge(sc_mm, a + 1)
            dve.tensor_reduce(neg_max[:, a, :], scores_of(a)[:, :].rearrange("p (c n) -> p c n", c=2)[:, :, 0:n],
                              AX.X, ALU.max, negate=True).then_inc(mx_v, 1)
            dve.wait_ge(mx_v, a + 1)
            dve.tensor_scalar(neg_max[:, a, :], neg_max[:, a, :], QK_DIM ** -0.5, None, ALU.mult).then_inc(mx_done, 1)

        def difference(a):
            n = KEY_TILES[a // HEADS] * P
            dve.wait_ge(ex_done, a + 1)
            dve.reciprocal(exp_r[:, a, :], exp_sum[:, a, :]).then_inc(pd_v, 1)
            dve.wait_ge(pd_v, 3 * a + 1)
            dve.tensor_tensor(exp_r[:, a, 1:2], exp_r[:, a, 1:2], neg_lam[:, :], ALU.mult).then_inc(pd_v, 1)
            dve.tensor_scalar(probs[a % 2][:, 0, 0:n], probs[a % 2][:, 0, 0:n], exp_r[:, a, 0:1], None, ALU.mult).then_inc(pd_v, 1)
            dve.wait_ge(pd_v, 3 * a + 3)
            dve.scalar_tensor_tensor(out=probs[a % 2][:, 0, 0:n], in0=probs[a % 2][:, 1, 0:n], scalar=exp_r[:, a, 1:2],
                                     in1=probs[a % 2][:, 0, 0:n], op0=ALU.mult, op1=ALU.add).then_inc(pd_rdy, 1)

        for a in range(ATT_UNITS + 3):
            if a < ATT_UNITS:
                score_max(a)
            if 1 <= a <= ATT_UNITS:
                difference(a - 1)
            if a >= HEADS + 2 and (a - 2) % HEADS == 0:
                t = (a - 2) // HEADS - 1
                dve.wait_ge(o_sq, t + 1)
                dve.tensor_reduce(head_ss[:, t, :], sq_o[:, :].rearrange("p (g n) -> p g n", n=P), AX.X, ALU.add).then_inc(o_red, 1)
        dve.wait_ge(o_red, TILES)
        dve.tensor_scalar(head_ss[:, :, :], head_ss[:, :, :], 1.0 / P, EPS, ALU.mult, ALU.add).then_inc(o_v, 1)
        dve.wait_ge(o_std, 1)
        dve.reciprocal(head_rstd[:, :, :], head_rstd[:, :, :]).then_inc(o_v, 1)
        dve.wait_ge(o_v, 2)

        def mix(t):
            o = mixed[:, t, :].rearrange("p (g n) -> p g n", n=P)
            o4 = mixed[:, t, :].rearrange("p (s g n) -> p s g n", s=2, n=P)
            dve.tensor_tensor(o, o, head_rstd[:, t, :].unsqueeze(2).to_broadcast([P, 8, P]), ALU.mult).then_inc(mix_v, 1)
            dve.wait_ge(hg_act, t + 1)
            dve.tensor_tensor(hg_sig[t % 2][:, :], hg_sig[t % 2][:, :], hg[t % 2][:, :], ALU.mult).then_inc(mix_v, 1)
            dve.wait_ge(mix_v, 3 * t + 2)
            dve.tensor_tensor(o4, o4, norm_w[:, :, :].unsqueeze(2).to_broadcast([P, 2, 4, P]), ALU.mult).then_inc(mix_v, 1)
            dve.wait_ge(mix_v, 3 * t + 3)
            dve.tensor_tensor(mixed[:, t, 0:512], mixed[:, t, 0:512], hg_sig[t % 2][:, :], ALU.mult).then_inc(mix_rdy, 1)

        def mix_low(t):
            dve.wait_ge(mth_done, t + 1)
            dve.tensor_tensor(mtl[t % 2][:, :, :], pair[2 + t % 2][:, :].rearrange("p (k n) -> p k n", k=KT),
                              mth[t % 2][:, :, :].bitcast(F32), ALU.subtract).then_inc(mtl_done, 1)

        mix(0)
        for k in range(KT):
            dve.wait_ge(woh_done, k + 1)
            dve.tensor_tensor(wol[:, k, :], wo_raw[k % 2][:, :], woh[:, k, :].bitcast(F32), ALU.subtract).then_inc(wol_done, 1)
            if k == 3:
                mix(1)
            if k == 6:
                mix_low(0)
        for t in range(TILES):
            if t + 1 < TILES:
                mix_low(t + 1)
            if t + 2 < TILES:
                mix(t + 2)
            dve.wait_ge(wo_mm, t + 1)
            dve.wait_ge(xa_in[t % 2], 16 * (t // 2 + 1))
            dve.tensor_tensor(mixed[:, t, :], pair[t % 2][:, :], x_again[t % 2][:, :], ALU.add).then_inc(h_done, 1)
        dve.wait_ge(h_sq, TILES)
        dve.tensor_scalar(stat2[:, :], stat2[:, :], 1.0 / D, EPS, ALU.mult, ALU.add).then_inc(h_v, 1)
        dve.wait_ge(h_std, 1)
        dve.reciprocal(rstd2[:, :], rstd2[:, :]).then_inc(h_v, 1)
        dve.wait_ge(h_v, 2)
        dve.wait_ge(norm2_in, 32)
        for t in range(TILES):
            if t >= 2:
                dve.wait_ge(xt_out[t % 2], 16 * (t // 2))
                dve.wait_ge(xtt_mm, t - 1)
            dve.scalar_tensor_tensor(out=xt[t % 2][:, :], in0=mixed[:, t, :], scalar=rstd2[:, t:t + 1],
                                     in1=norm2_bc[:, :], op0=ALU.mult, op1=ALU.mult).then_inc(xt_done, 1)
        dve.wait_ge(lg_mm, TILES)
        lg = PA[:, 0:TILES * EXPERTS].rearrange("p (t e) -> p t e", e=EXPERTS)
        dve.tensor_reduce(lmax[:, :], lg, AX.X, ALU.max).then_inc(rt_v, 1)
        dve.memset(aff[:, :, :], -1.0).then_inc(rt_v, 1)
        dve.wait_ge(rt_v, 2)
        dve.tensor_tensor(logit[:, :, :], lg, lmax[:, :].unsqueeze(2).to_broadcast([P, TILES, EXPERTS]), ALU.subtract).then_inc(rt_v, 1)
        dve.wait_ge(rt_exp, 1)
        dve.tensor_reduce(lsum[:, :], lexp[:, :, :], AX.X, ALU.add).then_inc(rt_v, 1)
        dve.wait_ge(rt_v, 4)
        dve.reciprocal(lsum[:, :], lsum[:, :]).then_inc(rt_v, 1)
        dve.wait_ge(rt_v, 5)
        for at, t0, n in ((0, PROMPT_TILES, 4), (32, 0, PROMPT_TILES)):
            dve.tensor_tensor(aff[:, 0:n, at:at + EXPERTS], lexp[:, t0:t0 + n, :],
                              lsum[:, t0:t0 + n].unsqueeze(2).to_broadcast([P, n, EXPERTS]), ALU.mult).then_inc(rt_v, 1)
        dve.memset(slot_gate[:, :], 0.0).then_inc(rt_v, 1)
        dve.memset(slot_token[:, :], 0.0).then_inc(top_v, 1)
        dve.wait_ge(rt_t, 1)
        dve.tensor_copy(aff_t[0][:, :], PB[0:48, 0:SAMPLE]).then_inc(top_v, 1)
        n = 2
        for r in range(CAP_S // 8):
            dve.wait_ge(top_v, n)
            cols = slice(8 * r, 8 * r + 8)
            dve.max(top[:, cols], aff_t[r % 2][:, :]).then_inc(top_v, 1)
            dve.wait_ge(top_v, n + 1)
            dve.max_index(top_i[:, cols], top[:, cols], aff_t[r % 2][:, :]).then_inc(top_v, 1)
            dve.match_replace(aff_t[(r + 1) % 2][:, :], top[:, cols], aff_t[r % 2][:, :], -2.0).then_inc(top_v, 1)
            n += 3
        dve.wait_ge(top_v, n)
        dve.tensor_copy(slot_gate[0:16, 0:CAP_S], top[0:16, :]).then_inc(top_v, 1)
        dve.tensor_copy(slot_gate[32:48, CAP_S:SLOTS], top[32:48, 0:CAP_P]).then_inc(top_v, 1)
        dve.tensor_copy(slot_token[0:16, 0:CAP_S], top_i[0:16, :]).then_inc(top_v, 1)
        dve.tensor_copy(slot_token[32:48, CAP_S:SLOTS], top_i[32:48, 0:CAP_P]).then_inc(top_v, 1)
        n += 4
        dve.wait_ge(top_v, n)
        dve.tensor_scalar(slot_token[0:16, 0:CAP_S], slot_token[0:16, 0:CAP_S], float(PROMPT), None, ALU.add).then_inc(top_v, 1)
        n += 1
        assert n == 3 * (CAP_S // 8) + 7
        dve.wait_ge(rt_t, 2)
        for o, dst in ((0, token), (64, gates)):
            dve.tensor_copy(dst[0:CAP_S, :], PC[0:CAP_S, o:o + 16])
            dve.tensor_copy(dst[CAP_S:SLOTS, :], PC[CAP_S:SLOTS, o + 32:o + 48]).then_inc(route_done, 1)

        H3 = (PB[:, 0:512], PB[:, 512:1024])
        TB = (PC[:, 0:512], PC[:, 512:1024])

        def rows_low(j, value):
            dve.wait_ge(th_done, value)
            dve.tensor_tensor(xel[:, 4 * j:4 * j + 4, :], TB[j][:, 0:4 * SLOTS].rearrange("p (k n) -> p k n", k=4),
                              xeh[:, 4 * j:4 * j + 4, :].bitcast(F32), ALU.subtract).then_inc(tl_done, 1)

        def chunk_low(e, c):
            n = chunk_size(c % CHUNKS)
            dve.wait_ge(ch_done, e * CHUNKS + (c + 1))
            dve.tensor_tensor(cl[c % SPLIT][:, 0:n], ring[c % RING][:, 0:n], ch[c % SPLIT][:, 0:n].bitcast(F32),
                              ALU.subtract).then_inc(cl_done, 1)

        def expert(e, last):
            for cc in range(2, CHUNKS + 2):
                if cc < CHUNKS or not last:
                    chunk_low(e, cc)
                c = cc - 2
                if c % 2 == 1 and c < 2 * NFC:
                    fc = c // 2
                    dve.wait_ge(silu_done, e * NFC + (fc + 1))
                    dve.wait_ge(used, e * CHUNKS + (c + 1 + SPLIT))
                    dve.tensor_tensor(hid[:, fc * FC:(fc + 1) * FC], H3[fc % 2][0:SLOTS, 0:FC], silu[fc % 2][:, :],
                                      ALU.mult).then_inc(hid_done, 1)
                if c >= 2 and c % 2 == 0 and c // 2 - 1 < NFC:
                    fc = c // 2 - 1
                    k0, k1 = (TILES_AFTER[fc - 1] if fc else 0), TILES_AFTER[fc]
                    dve.wait_ge(th_done, e * T_PER_EXPERT + (3 + fc))
                    dve.tensor_tensor(hid_l[:, k0:k1, :],
                                      TB[fc % 2][:, 0:(k1 - k0) * SLOTS].rearrange("p (k n) -> p k n", k=k1 - k0),
                                      hid_h[:, k0:k1, :].bitcast(F32), ALU.subtract).then_inc(tl_done, 1)
                if not last and c in (2 * NFC + 2, 2 * NFC + 3):
                    j = c - 2 * NFC - 2
                    rows_low(j, e * T_PER_EXPERT + (3 + NFC + j))

        dve.sem_inc(hid_done, 2)
        rows_low(0, 1)
        rows_low(1, 2)
        chunk_low(0, 0)
        chunk_low(0, 1)
        with dve.Fori(0, EXPERTS - 1) as e:
            expert(e, False)
        expert(EXPERTS - 1, True)

    @block.gpsimd
    def _(pool):
        for h in range(HEADS):
            pool.wait_ge(lu_mm, PER_HEAD * (h + 1))
            for d in range(2):
                hd = d * 4 + h
                pool.wait_ge(e_done, 2 * h + d + 1)
                k_factor = e2[0][:, :] if d == 0 else gate[:, hd, :]
                q_factor = gate[:, hd, :] if d == 0 else e2[1][:, :]
                pool.tensor_tensor(keys[:, hd, :], keys[:, hd, :], k_factor, ALU.mult).then_inc(fac, 1)
                pool.wait_ge(fac, 4 * h + 2 * d + 1)
                pool.tensor_tensor(gate[:, hd, :], q_fm[:, h, :], q_factor, ALU.mult).then_inc(fac, 1)

        def gather(e):
            pool.indirect_dma_start(out=xe[:, :], out_offset=None, in_=xt_d,
                                    in_offset=bass.IndirectOffsetOnAxis(ap=token[:, e:e + 1], axis=0),
                                    bounds_check=T - 1).then_inc(xe_in, 16)

        pool.wait_ge(route_done, 2)
        pool.sem_inc(y_free, 1)
        for i in range(2):
            pool.wait_ge(xt_out[i], 16 * (TILES // 2))
        pool.wait_ge(h_out, 16 * TILES)
        gather(0)
        for e in range(EXPERTS):
            if e + 1 < EXPERTS:
                pool.wait_ge(t_mm, e * T_PER_EXPERT + 2)
                gather(e + 1)
            pool.wait_ge(y_ev, e + 2)
            pool.indirect_dma_start(out=out, out_offset=bass.IndirectOffsetOnAxis(ap=token[:, e:e + 1], axis=0),
                                    in_=y_sb[:, :], in_offset=None, bounds_check=T - 1,
                                    compute_op=ALU.add).then_inc(y_out, 16)
            pool.wait_ge(y_out, 16 * (e + 1))
            pool.sem_inc(y_free, 1)

    moe.close()
    perm.close()


def constants():
    ident = np.eye(P, dtype=np.float32)
    j, i = np.arange(P)[:, None], np.arange(P)[None, :]
    masks = np.zeros((P, 2 * NL, P), np.float32)
    for l, m in enumerate(LEVELS):
        same = j // (2 * m) == i // (2 * m)
        j_first, i_first = j // m % 2 == 0, i // m % 2 == 0
        masks[:, l, :] = same & j_first & ~i_first
        masks[:, NL + l, :] = same & ~j_first & i_first
    half = QK_DIM // 8
    inv_freq = (1.0 / (500000.0 ** (np.arange(0, 2 * half, 2, dtype=np.float32) / (2 * half)))).astype(np.float32)
    position = np.concatenate([np.arange(PROMPT), np.arange(SAMPLE)]).astype(np.float32)
    angle = (position[:, None] * inv_freq[None, :]).reshape(TILES, P, half).transpose(1, 0, 2)
    return ident, masks, np.ascontiguousarray(np.cos(angle)), np.ascontiguousarray(np.sin(angle))


def kernel(**inputs):
    import concourse.bacc as bacc
    from concourse.bass_utils import run_bass_kernel_spmd

    nc = bacc.Bacc("TRN2", target_bir_lowering=False, num_devices=1)
    ident, masks, cos, sin = constants()
    given = {k: np.asarray(v) for k, v in inputs.items()}
    arrays = {
        "x": np.concatenate([given["x_prompt"][0], given["x_sample"][0]], axis=0),
        "norm1": given["norm1_w"], "w_in": given["w_in"][0],
        "lbf": given["hg_lb_fwd"], "lbb": given["hg_lb_bwd"], "hgw": given["hg_norm_w"],
        "qw": given["q_norm_w"], "kw": given["k_norm_w"],
        "lams": np.concatenate([given[f"lambda_{n}"] for n in ("q1", "k1", "q2", "k2")], axis=0)[None],
        "subw": given["subln_w"], "w_out": given["w_out"][0], "norm2": given["norm2_w"],
        "rw": given["router_w"][0], "w1": given["w1"][0], "w3": given["w3"][0], "w2": given["w2"][0],
        "ident_c": ident, "masks_c": masks, "cos_c": cos, "sin_c": sin,
    }
    arrays = {k: np.ascontiguousarray(v) for k, v in arrays.items()}
    aps = [nc.dram_tensor(n, a.shape, mybir.dt.from_np(a.dtype), kind="ExternalInput").ap() for n, a in arrays.items()]
    flat = {"norm1", "hgw", "qw", "kw", "subw", "norm2"}
    aps = [ap[0, :] if n in flat else ap[0] if n == "lams" else ap for n, ap in zip(arrays, aps)]
    out = nc.dram_tensor("y", (T, D), F32, kind="ExternalOutput").ap()
    tm_d = nc.dram_tensor("projected", (T, 5 * HW), F32).ap()
    xt_d = nc.dram_tensor("moe_rows", (T, D), F32).ap()
    build(nc, *aps, out, tm_d, xt_d)
    y = run_bass_kernel_spmd(nc, [arrays], core_ids=[0]).results[0]["y"]
    return y[None, :PROMPT], y[None, PROMPT:]
```

```python
from contextlib import ExitStack

import numpy as np

import concourse.bass as bass
from concourse import mybir

F32 = mybir.dt.float32
F32R = mybir.dt.float32r
U32 = mybir.dt.uint32
U8 = mybir.dt.uint8
ALU = mybir.AluOpType
ACT = mybir.ActivationFunctionType
AX = mybir.AxisListType

P = 128
D = 1024
KT = D // P
PROMPT, SAMPLE = 256, 512
T = PROMPT + SAMPLE
TILES = T // P
PROMPT_TILES = PROMPT // P
FIRST_TILE = [0, 0, 2, 2, 2, 2]
KEY_TILES = [2, 2, 4, 4, 4, 4]
HEADS = 4
HW = HEADS * P
EPS = 1e-6
QK_DIM = 64
LAM_INIT = 0.2
HC = 256
PIECES = 8 * HW // HC
FM_PIECES = 3 * HW // HC
FM_UNITS = 3 * HEADS
TM_UNITS = (PIECES - FM_PIECES) * TILES
LEVELS = [64, 32, 16, 8, 4, 2, 1]
NL = len(LEVELS)
PER_HEAD = 1 + NL
LUS = HEADS * PER_HEAD
LAG = 3
LU_AT = [LAG + i * (TM_UNITS - LAG) // LUS for i in range(LUS)]
STAGES = 4
STATE_UNITS = [(0, 0), (1, 1), (0, 2), (1, 5), (0, 3), (1, 4), (0, 4), (1, 3)]
ATT_UNITS = TILES * HEADS
WO_AT = TILES + 1
NORM_AT = ATT_UNITS
PROBS = 3

EXPERTS = 16
FF = 2816
FT = FF // P
CAP_P, CAP_S = 2 * PROMPT // EXPERTS, 2 * SAMPLE // EXPERTS
SLOTS = CAP_P + CAP_S
FC = 352
NFC = FF // FC
W2_KT = [3, 3, 3, 3, 3, 3, 2, 2]
W2_AT = [sum(W2_KT[:j]) for j in range(len(W2_KT))]
CHUNKS = 2 * NFC + len(W2_KT)
RING = 6
SPLIT = 3
EARLY = 2
CHUNK = 3 * D
TILES_AFTER = [FC * (c + 1) // P for c in range(NFC)]
T_PER_EXPERT = NFC + 2


def build(nc, x, norm1, w_in, lbf, lbb, hgw, qw, kw, lams, subw, w_out, norm2, rw, w1, w3, w2,
          ident_d, masks_d, cos_d, sin_d, out, tm_d, xt_d):
    perm = ExitStack()

    def sb(stack, name, shape, dt=F32, side="left"):
        return stack.enter_context(nc.sbuf_tensor(name, shape, dt, side=side))

    def sem(name):
        return perm.enter_context(nc.semaphore(name))

    ident = sb(perm, "ident", [P, P])
    norm_w = sb(perm, "head_norm_w", [P, 2, P])
    qk_w = sb(perm, "qk_norm_w", [P, 2, QK_DIM])
    cos = sb(perm, "cos", [P, TILES, 8])
    sin = sb(perm, "sin", [P, TILES, 8])
    lam4 = sb(perm, "lambda_rows", [P, 4, QK_DIM])
    lam_p = sb(perm, "lambda_products", [P, 2, QK_DIM])
    lam_s = sb(perm, "lambda_sums", [P, 2])
    neg_lam = sb(perm, "neg_lambda", [P, 1])
    lb_raw = sb(perm, "lb_raw", [P, 2, 2, HEADS])
    lb_max = sb(perm, "lb_max", [P, 2, HEADS])
    lb = sb(perm, "lb", [P, 2, HEADS])
    one_minus_lb = sb(perm, "one_minus_lb", [P, 2, HEADS])
    token = sb(perm, "token", [SLOTS, EXPERTS], U32)
    gates = sb(perm, "gates", [SLOTS, EXPERTS])
    stat1 = sb(perm, "stat1", [P, TILES])
    rstd1 = sb(perm, "rstd1", [P, TILES])
    qk_ss = sb(perm, "qk_ss", [P, TILES, 16])
    qk_rstd = sb(perm, "qk_rstd", [P, TILES, 16])
    head_ss = sb(perm, "head_ss", [P, TILES, 8])
    head_rstd = sb(perm, "head_rstd", [P, TILES, 8])
    stat2 = sb(perm, "stat2", [P, TILES])
    rstd2 = sb(perm, "rstd2", [P, TILES])
    neg_max = sb(perm, "neg_max", [P, ATT_UNITS, 2])
    exp_sum = sb(perm, "exp_sum", [P, ATT_UNITS, 2])
    exp_r = sb(perm, "exp_r", [P, ATT_UNITS, 2])
    chunk_decay = sb(perm, "chunk_decay", [P, 8, TILES])

    left0, right = ExitStack(), ExitStack()
    raw_w = [sb(left0, f"raw_w{i}", [P, KT, HC]) for i in range(2)]
    stage = [sb(left0, f"stage{i}", [P, HC]) for i in range(STAGES)]
    sq = [sb(left0, f"sq{i}", [P, HC]) for i in range(2)]
    first = ExitStack()
    x_in = sb(first, "x_in", [P, TILES, D])
    x_scaled = sb(first, "x_scaled", [P, TILES, D])
    norm1_bc = sb(first, "norm1_bc", [P, D])
    first.close()
    left0.close()
    mixed_stack = ExitStack()
    mixed = sb(mixed_stack, "mixed", [P, TILES, D])
    gla = ExitStack()
    gate = sb(gla, "gate", [P, 8, T])
    keys = sb(gla, "keys", [P, 8, T])
    q_fm = sb(gla, "q_fm", [P, HEADS, T])
    att_t = sb(gla, "att_t", [P, HEADS, T])
    btot = sb(gla, "btot", [P, 8, TILES])
    e2 = [sb(gla, f"e2_{i}", [P, T]) for i in range(2)]
    lev = ExitStack()
    masks = sb(lev, "masks", [P, NL, P], U8)
    before = ExitStack()
    masks_f = sb(before, "masks_f", [P, NL, P])
    restart = sb(before, "restart", [P, T])
    lev_tmp = sb(before, "lev_tmp", [P, T])
    before.close()
    xl = [sb(lev, f"level{i}", [P, 2, T]) for i in range(3)]
    lev.close()
    states = sb(gla, "states", [P, len(STATE_UNITS), HW])
    gla.close()
    xh = sb(right, "x_high", [P, KT, T], F32R, "right")
    xlo = sb(right, "x_low", [P, KT, T], F32R, "right")
    wh = [sb(right, f"w_high{i}", [P, KT, HC], F32R, "right") for i in range(2)]
    wl = [sb(right, f"w_low{i}", [P, KT, HC], F32R, "right") for i in range(2)]
    right.close()
    att = ExitStack()
    v_tm = sb(att, "v_tm", [P, TILES, HW], side="right")
    av = sb(att, "av", [P, TILES, HW], side="right")
    qt = sb(att, "q_t", [P, HEADS, T], side="right")
    kt_ = sb(att, "k_t", [P, HEADS, T], side="right")
    qk = [sb(att, f"qk{i}", [P, 2 * HW], side="right") for i in range(2)]
    rope_t = sb(att, "rope_t", [P, 4, 16, 8], side="right")
    probs = [sb(att, f"probs{i}", [P, 2, 512], side="right") for i in range(PROBS)]
    probs_t = [sb(att, f"probs_t{i}", [P, 512], side="right") for i in range(2)]
    kdec_tm = [sb(att, f"kdec_tm{i}", [P, HW], side="right") for i in range(2)]
    sq_o = sb(att, "sq_o", [P, D], side="right")
    att.close()
    outp = ExitStack()
    woh = sb(outp, "wo_high", [P, KT, D], F32R)
    wol = sb(outp, "wo_low", [P, KT, D], F32R)
    wo_raw = [sb(outp, f"wo_raw{i}", [P, D]) for i in range(2)]
    hg = [sb(outp, f"hg{i}", [P, HW]) for i in range(2)]
    x_again = [sb(outp, f"x_again{i}", [P, D]) for i in range(2)]
    mth = [sb(outp, f"mix_high{i}", [P, KT, P], F32R) for i in range(2)]
    mtl = [sb(outp, f"mix_low{i}", [P, KT, P], F32R) for i in range(2)]
    norm2_bc = sb(outp, "norm2_bc", [P, D])
    rw_sb = sb(outp, "router_w", [P, KT, EXPERTS])
    outp.close()
    rout = ExitStack()
    xtt = [sb(rout, f"xt_t{i}", [P, KT, P]) for i in range(2)]
    lg_t = sb(rout, "logits_t", [EXPERTS, T])
    lmax = sb(rout, "logit_max", [P, TILES])
    logit = sb(rout, "logit", [P, TILES, EXPERTS])
    lexp = sb(rout, "logit_exp", [P, TILES, EXPERTS])
    lsum = sb(rout, "logit_sum", [P, TILES])
    aff = sb(rout, "affinity", [P, 4, 48])
    aff_t = [sb(rout, f"affinity_t{i}", [48, SAMPLE]) for i in range(2)]
    top = sb(rout, "top_values", [48, CAP_S])
    top_i = sb(rout, "top_tokens", [48, CAP_S], U32)
    slot_gate = sb(rout, "slot_gate", [48, SLOTS])
    slot_token = sb(rout, "slot_token", [48, SLOTS])
    rout.close()
    mixed_stack.close()
    moe = ExitStack()
    ring = [sb(moe, f"ring{i}", [P, CHUNK], side="right") for i in range(RING)]
    silu = [sb(moe, f"silu{i}", [SLOTS, FC]) for i in range(2)]
    hid = sb(moe, "hid", [SLOTS, FF])
    hid_h = sb(moe, "hid_high", [P, FT, SLOTS], F32R)
    hid_l = sb(moe, "hid_low", [P, FT, SLOTS], F32R)
    xe = sb(moe, "xe", [SLOTS, D])
    xeh = sb(moe, "xe_high", [P, KT, SLOTS], F32R)
    xel = sb(moe, "xe_low", [P, KT, SLOTS], F32R)
    y_sb = sb(moe, "y_rows", [SLOTS, D])
    ch = [sb(moe, f"chunk_high{i}", [P, CHUNK], F32R) for i in range(SPLIT)]
    cl = [sb(moe, f"chunk_low{i}", [P, CHUNK], F32R) for i in range(SPLIT)]

    pair = [perm.enter_context(nc.psum_tensor(f"pair{i}", [P, 1024], F32)) for i in range(4)]
    PA, PB, PC, PD = pair

    consts_in = sem("consts_in")
    lb_in = sem("lb_in")
    masks_in = sem("masks_in")
    masks_done = sem("masks_done")
    norm2_in = sem("norm2_in")
    x_tile_in = [sem(f"x_tile_in{i}") for i in range(TILES)]
    w_in_sem = [sem(f"w_piece_in{i}") for i in range(2)]
    setup_v = sem("setup_v")
    setup_a = sem("setup_a")
    x_sq = sem("x_sq")
    x_std = sem("x_std")
    x_rstd = sem("x_rstd")
    xs_ready = sem("xs_ready")
    x_t = sem("x_t")
    xh_done = sem("xh_done")
    xl_done = sem("xl_done")
    wh_done = sem("w_high_done")
    wl_done = sem("w_low_done")
    fm_mm = sem("fm_mm")
    fm_act = sem("fm_act")
    q_done = sem("q_done")
    f_done = sem("f_done")
    k_done = sem("k_done")
    ln_done = sem("ln_done")
    scan_v = sem("scan_v")
    tm_mm = sem("tm_mm")
    tm_ev = sem("tm_ev")
    stage_full = sem("stage_full")
    stage_out = [sem(f"stage_out{i}") for i in range(STAGES)]
    sq_full = sem("sq_full")
    sq_used = sem("sq_used")
    x_sub = sem("level_sub")
    x_exp = sem("level_exp")
    x_rdy = sem("level_ready")
    lu_mm = sem("level_mm")
    lu_ev = sem("level_merged")
    e2_done = sem("suffix_decays_done")
    e_done = sem("decays_done")
    decay_done = sem("chunk_decay_done")
    fac = sem("factors_done")
    v_in = sem("v_in")
    av_in = sem("av_in")
    qk_in = [sem(f"qk_in{i}") for i in range(2)]
    qk_std = sem("qk_std")
    qk_v = sem("qk_v")
    qk_rdy = sem("qk_ready")
    qk_t = sem("qk_transposed")
    qk_ev = sem("qk_evacuated")
    kd_t = sem("kdec_transposed")
    kd_ev = sem("kdec_evacuated")
    u_mm = sem("update_mm")
    s_done = sem("state_done")
    sc_mm = sem("scores_mm")
    mx_v = sem("score_max_v")
    mx_done = sem("score_max")
    ex_done = sem("score_exp")
    pd_v = sem("probs_v")
    pd_rdy = sem("probs_ready")
    pt_mm = sem("probs_transposed")
    pt_ev = sem("probs_t_evacuated")
    pv_mm = sem("pv_mm")
    ao_ev = sem("attention_out")
    go_mm = sem("gla_mm")
    go_ev = sem("gla_out")
    o_sq = sem("out_squares")
    o_red = sem("out_squares_used")
    o_std = sem("out_std")
    o_v = sem("out_v")
    wo_in = [sem(f"wo_in{i}") for i in range(2)]
    woh_done = sem("wo_high_done")
    wol_done = sem("wo_low_done")
    xa_in = [sem(f"x_again_in{i}") for i in range(2)]
    hg_in = [sem(f"hg_in{i}") for i in range(2)]
    hg_act = sem("hg_silu")
    mix_v = sem("mix_v")
    mix_rdy = sem("mix_ready")
    mt_mm = sem("mix_transposed")
    mth_done = sem("mix_high_done")
    mtl_done = sem("mix_low_done")
    wo_mm = sem("wo_mm")
    h_done = sem("h_done")
    h_sq = sem("h_squares")
    h_out = [sem(f"h_out{t}") for t in range(TILES)]
    h_std = sem("h_std")
    h_v = sem("h_v")
    xt_done = sem("xt_done")
    xt_out = sem("xt_out")
    xtt_mm = sem("xt_transposed")
    xtt_ev = sem("xt_t_evacuated")
    lg_mm = sem("logits_t_mm")
    lg_ev = sem("logits_t_evacuated")
    lg_done = sem("logits_done")
    rt_v = sem("router_v")
    rt_exp = sem("router_exp")
    rt_t = sem("router_transposed")
    top_v = sem("top_v")
    route_done = sem("route_done")
    raw_in = [sem(f"chunk_in{i}") for i in range(RING)]
    ch_done = sem("chunk_high_done")
    cl_done = sem("chunk_low_done")
    early_low = sem("early_chunk_low_done")
    used = sem("chunks_used")
    silu_done = sem("silu_done")
    hid_done = sem("hid_done")
    t_mm = sem("t_mm")
    th_done = sem("t_high_done")
    tl_done = sem("t_low_done")
    xe_in = sem("xe_in")
    y_ev = sem("y_evacuated")
    y_out = sem("y_scattered")
    y_free = sem("y_rows_free")

    NCONST = 9

    def tile(t):
        return slice(t * P, (t + 1) * P)

    def level_of(i):
        h, j = divmod(i, PER_HEAD)
        return (h, None) if j == 0 else (h, j - 1)

    def levels_to(i):
        return i + 1 - (i // PER_HEAD + 1)

    def split_slot_free(hc):
        old = hc - 2
        return (fm_mm, 2 * old + 2) if old < FM_PIECES else (tm_mm, TILES * (old - FM_PIECES + 1))

    def scores_of(a):
        return pair[a % 2]

    def logits_bank(t):
        return PA[0:EXPERTS, (t % 2) * 512:(t % 2) * 512 + P]

    def chunk_view(buf, c):
        if c < 2 * NFC:
            return buf[:, 0:KT * FC].rearrange("p (k n) -> p k n", k=KT)
        k = W2_KT[c - 2 * NFC]
        return buf[:, 0:k * D].rearrange("p (k n) -> p k n", k=k)

    def chunk_size(c):
        return KT * FC if c < 2 * NFC else W2_KT[c - 2 * NFC] * D

    def load_chunk(sp, e, c, ahead=0):
        if c < 2 * NFC:
            w, c0 = (w1, w3)[c % 2], c // 2 * FC
            src = w.rearrange("e d n -> (e d) n")[bass.ds(e * D + ahead * D, D), c0:c0 + FC]
        else:
            j = c - 2 * NFC
            src = w2.rearrange("e f n -> (e f) n")[bass.ds(e * FF + (ahead * FF + W2_AT[j] * P), W2_KT[j] * P), :]
        src = src.rearrange("(k p) n -> p k n", p=P)
        sp.dma_start(chunk_view(ring[c % RING], c), src).then_inc(raw_in[c % RING], 16)

    block = perm.enter_context(nc.Block())

    @block.sync
    def _(sp):
        with nc.allow_non_contiguous_dma(reason="small constants in a transposed layout"):
            sp.dma_start(ident[:, :], ident_d).then_inc(consts_in, 16)
            for t in range(TILES):
                sp.dma_start(x_in[:, t, :], x[tile(t), :]).then_inc(x_tile_in[t], 16)
                if t == 0:
                    sp.dma_start(norm1_bc[:, :], norm1.partition_broadcast(P)).then_inc(consts_in, 16)
            for hc in range(2):
                sp.dma_start(raw_w[hc][:, :, :],
                             w_in[:, hc * HC:(hc + 1) * HC].rearrange("(k p) n -> p k n", p=P)).then_inc(w_in_sem[hc], 16)
            for i, d_lb in enumerate((lbf, lbb)):
                for r in range(2):
                    sp.dma_start(lb_raw[:, i, r, :], d_lb[r, :].rearrange("(h k) -> k h", k=P)).then_inc(lb_in, 16)
            for i, w in enumerate((hgw, subw)):
                sp.dma_start(norm_w[:, i, :], w.partition_broadcast(P)).then_inc(consts_in, 16)
            for i, w in enumerate((qw, kw)):
                sp.dma_start(qk_w[:, i, :], w.partition_broadcast(P)).then_inc(consts_in, 16)
            sp.dma_start(cos[:, :, :], cos_d).then_inc(consts_in, 16)
            sp.dma_start(sin[:, :, :], sin_d).then_inc(consts_in, 16)
            sp.dma_start(lam4[:, :, :], lams.partition_broadcast(P)).then_inc(consts_in, 16)
            sp.wait_ge(x_t, TILES)
            sp.dma_start(masks_f[:, :, :], masks_d).then_inc(masks_in, 16)
            for hc in range(PIECES):
                if hc + 2 < PIECES:
                    sp.wait_ge(wl_done, hc + 1)
                    c0 = (hc + 2) * HC
                    sp.dma_start(raw_w[hc % 2][:, :, :],
                                 w_in[:, c0:c0 + HC].rearrange("(k p) n -> p k n", p=P)).then_inc(w_in_sem[hc % 2], 16)
                if hc >= FM_PIECES:
                    for t in range(TILES):
                        n = (hc - FM_PIECES) * TILES + t
                        sp.wait_ge(stage_full, n + 1)
                        c0 = (hc - FM_PIECES) * HC
                        sp.dma_start(tm_d[tile(t), c0:c0 + HC], stage[n % STAGES][:, :]).then_inc(stage_out[n % STAGES], 16)
            sp.wait_ge(tm_mm, TM_UNITS)
            for i in range(STAGES):
                sp.wait_ge(stage_out[i], 16 * (TM_UNITS // STAGES))
            for t in range(TILES):
                if t >= 2:
                    sp.wait_ge(qk_t, t - 1)
                sp.dma_start(qk[t % 2][:, :], tm_d[tile(t), 2 * HW:4 * HW]).then_inc(qk_in[t % 2], 16)
                if t == 1:
                    sp.dma_start(v_tm[:, :, :], tm_d[:, 0:HW].rearrange("(t p) n -> p t n", p=P)).then_inc(v_in, 16)
                    sp.dma_start(av[:, :, :], tm_d[:, 4 * HW:5 * HW].rearrange("(t p) n -> p t n", p=P)).then_inc(av_in, 16)
            sp.wait_ge(go_mm, TILES)
            for k in range(2):
                sp.dma_start(wo_raw[k % 2][:, :], w_out[tile(k), :]).then_inc(wo_in[k % 2], 16)
            for k in range(2):
                sp.dma_start(hg[k][:, :], tm_d[tile(k), HW:2 * HW]).then_inc(hg_in[k], 16)
                sp.dma_start(x_again[k][:, :], x[tile(k), :]).then_inc(xa_in[k], 16)
            for k in range(2, KT):
                sp.wait_ge(wol_done, k - 1)
                sp.dma_start(wo_raw[k % 2][:, :], w_out[tile(k), :]).then_inc(wo_in[k % 2], 16)
            sp.wait_ge(o_red, TILES)
            sp.dma_start(norm2_bc[:, :], norm2.partition_broadcast(P)).then_inc(norm2_in, 16)
            sp.dma_start(rw_sb[:, :, :], rw.rearrange("(k p) e -> p k e", p=P)).then_inc(norm2_in, 16)
            for t in range(TILES):
                if t >= 1:
                    load_chunk(sp, 0, t - 1)
                if t + 2 < TILES:
                    sp.wait_ge(mix_rdy, t + 1)
                    sp.dma_start(hg[t % 2][:, :], tm_d[tile(t + 2), HW:2 * HW]).then_inc(hg_in[t % 2], 16)
                sp.wait_ge(h_done, t + 1)
                sp.dma_start(out[tile(t), :], mixed[:, t, :]).then_inc(h_out[t], 16)
                if t + 2 < TILES:
                    sp.dma_start(x_again[t % 2][:, :], x[tile(t + 2), :]).then_inc(xa_in[t % 2], 16)
            for c in range(TILES - 1, RING):
                load_chunk(sp, 0, c)
            for t in range(TILES):
                sp.wait_ge(xt_done, t + 1)
                sp.dma_start(xt_d[tile(t), :], mixed[:, t, :]).then_inc(xt_out, 16)
            for c in range(EARLY):
                sp.wait_ge(early_low, c + 1)
                load_chunk(sp, 0, c + RING)
            with sp.Fori(0, EXPERTS - 1) as e:
                for c in range(EARLY, CHUNKS + EARLY):
                    sp.wait_ge(cl_done, e * CHUNKS + (c + 1))
                    load_chunk(sp, e, (c + RING) % CHUNKS, (c + RING) // CHUNKS)
            for c in range(EARLY, CHUNKS - RING):
                sp.wait_ge(cl_done, (EXPERTS - 1) * CHUNKS + c + 1)
                load_chunk(sp, EXPERTS - 1, c + RING)

    @block.tensor
    def _(pe):
        def split_mm(dst, a_high, a_low, b_high, b_low, first, last):
            pe.matmul(dst, a_high, b_high, start=first, stop=False)
            pe.matmul(dst, a_high, b_low, start=False, stop=False)
            return pe.matmul(dst, a_low, b_high, start=False, stop=last)

        pe.wait_ge(consts_in, 16 * NCONST)
        for t in range(TILES):
            pe.wait_ge(xs_ready, t + 1)
            if t >= 2:
                pe.wait_ge(xl_done, t - 1)
            for k in range(KT):
                mm = pe.transpose(pair[2 + t % 2][:, tile(k)], x_scaled[:, t, tile(k)], ident[:, :])
            mm.then_inc(x_t, 1)
        pe.wait_ge(xl_done, TILES)
        for u in range(FM_UNITS):
            hc = u // 2
            if u % 2 == 0:
                pe.wait_ge(wl_done, hc + 1)
            if u >= 2:
                if u - 2 < HEADS:
                    pe.wait_ge(q_done, u - 1)
                else:
                    pe.wait_ge(fm_act, u - 1)
            dst = pair[u % 2]
            cols = slice((u % 2) * P, (u % 2 + 1) * P)
            for k in range(KT):
                for d0, d1, x0, x1 in ((0, SAMPLE, PROMPT, T), (512, 512 + PROMPT, 0, PROMPT)):
                    mm = split_mm(dst[:, d0:d1], wh[hc % 2][:, k, cols], wl[hc % 2][:, k, cols],
                                  xh[:, k, x0:x1], xlo[:, k, x0:x1], k == 0, k == KT - 1)
            mm.then_inc(fm_mm, 1)

        def token_major(n):
            hc, t = FM_PIECES + n // TILES, n % TILES
            if t == 0:
                pe.wait_ge(wl_done, hc + 1)
            if n >= 2:
                pe.wait_ge(tm_ev, n - 1)
            dst = PC[:, (n % 2) * 512:(n % 2) * 512 + HC]
            for k in range(KT):
                mm = split_mm(dst, xh[:, k, tile(t)], xlo[:, k, tile(t)], wh[hc % 2][:, k, :],
                              wl[hc % 2][:, k, :], k == 0, k == KT - 1)
            mm.then_inc(tm_mm, 1)

        def pairs_of_level(i):
            h, level = level_of(i)
            dst = pair[i % 2]
            if i < 2:
                pe.wait_ge(fm_act, FM_UNITS)
                pe.wait_ge(k_done, 8)
                pe.wait_ge(q_done, HEADS)
            else:
                pe.wait_ge(lu_ev, i - 1)
            if level is not None:
                pe.wait_ge(x_rdy, levels_to(i))
            for t in range(TILES):
                at = dst[:, t // 3 * 512 + t % 3 * P:t // 3 * 512 + t % 3 * P + P]
                if level is None:
                    pe.matmul(at, keys[:, h, tile(t)], q_fm[:, h, tile(t)], start=True, stop=False)
                    mm = pe.matmul(at, keys[:, 4 + h, tile(t)], q_fm[:, h, tile(t)], start=False, stop=True)
                else:
                    lv = xl[(levels_to(i) - 1) % 3]
                    mm = pe.matmul(at, lv[:, 0, tile(t)], lv[:, 1, tile(t)], start=True, stop=True)
            mm.then_inc(lu_mm, 1)

        for n in range(LU_AT[-1] + 3):
            if n < TM_UNITS:
                token_major(n)
            if n - 2 in LU_AT:
                pairs_of_level(LU_AT.index(n - 2))

        def updates(w):
            d, t = STATE_UNITS[w]
            pe.wait_ge(kd_ev, w + 1)
            if w == 0:
                pe.wait_ge(v_in, 16)
            if w >= 2:
                pe.wait_ge(s_done, w - 1)
            for h in range(HEADS):
                mm = pe.matmul(PD[:, (w % 2) * 512 + h * P:(w % 2) * 512 + (h + 1) * P],
                               kdec_tm[w % 2][:, tile(h)], v_tm[:, t, tile(h)], start=True, stop=True)
            mm.then_inc(u_mm, 1)

        pe.wait_ge(lu_ev, LUS)
        pe.wait_ge(tm_ev, TM_UNITS)
        for w in range(len(STATE_UNITS) + 1):
            if w < len(STATE_UNITS):
                d, t = STATE_UNITS[w]
                if w == 0:
                    pe.wait_ge(fac, 16)
                if w >= 2:
                    pe.wait_ge(kd_ev, w - 1)
                for h in range(HEADS):
                    mm = pe.transpose(PC[:, (w % 2) * 512 + h * P:(w % 2) * 512 + (h + 1) * P],
                                      keys[:, d * 4 + h, tile(t)], ident[:, :])
                mm.then_inc(kd_t, 1)
            if w < TILES:
                pe.wait_ge(qk_rdy, w + 1)
                if w >= 2:
                    pe.wait_ge(qk_ev, w - 1)
                for j in range(2 * HEADS):
                    mm = pe.transpose(pair[w % 2][:, tile(j)], qk[w % 2][:, tile(j)], ident[:, :])
                mm.then_inc(qk_t, 1)
            if w >= 1:
                updates(w - 1)

        def scores(a):
            t, h = divmod(a, HEADS)
            n = KEY_TILES[t] * P
            k0 = FIRST_TILE[t] * P
            if a < 2:
                pe.wait_ge(qk_ev, TILES)
            else:
                pe.wait_ge(ex_done, a - 1)
            for c in range(2):
                rows = slice(c * QK_DIM, (c + 1) * QK_DIM)
                mm = pe.matmul(scores_of(a)[:, c * 512:c * 512 + n], qt[rows, h, tile(t)],
                               kt_[rows, h, k0:k0 + n], start=True, stop=True)
            mm.then_inc(sc_mm, 1)

        def transpose_probs(a):
            t, h = divmod(a, HEADS)
            pe.wait_ge(pd_rdy, a + 1)
            if a < 2:
                pe.wait_ge(kd_ev, len(STATE_UNITS))
            else:
                pe.wait_ge(pt_ev, a - 1)
            for k in range(KEY_TILES[t]):
                mm = pe.transpose(PC[:, (a % 2) * 512 + k * P:(a % 2) * 512 + (k + 1) * P],
                                  probs[a % PROBS][:, 0, tile(k)], ident[:, :])
            mm.then_inc(pt_mm, 1)

        def values(a):
            t, h = divmod(a, HEADS)
            pe.wait_ge(pt_ev, a + 1)
            if a == 0:
                pe.wait_ge(av_in, 16)
                pe.wait_ge(s_done, len(STATE_UNITS))
            if h == 0 and t >= 1:
                pe.wait_ge(ao_ev, t)
            for k in range(KEY_TILES[t]):
                mm = pe.matmul(PD[:, tile(h)], probs_t[a % 2][:, tile(k)],
                               av[:, FIRST_TILE[t] + k, tile(h)], start=k == 0, stop=k == KEY_TILES[t] - 1)
            mm.then_inc(pv_mm, 1)

        def hgrn_out(t):
            if t >= 1:
                pe.wait_ge(go_ev, t)
            else:
                pe.wait_ge(s_done, len(STATE_UNITS))
                pe.wait_ge(lu_ev, LUS)
            for h in range(HEADS):
                dst = PD[:, 512 + h * P:512 + (h + 1) * P]
                terms = [(att_t[:, h, tile(t)], v_tm[:, t, tile(h)])]
                if (0, t - 1) in STATE_UNITS:
                    terms.append((gate[:, h, tile(t)], states[:, STATE_UNITS.index((0, t - 1)), tile(h)]))
                if (1, t + 1) in STATE_UNITS:
                    terms.append((gate[:, 4 + h, tile(t)], states[:, STATE_UNITS.index((1, t + 1)), tile(h)]))
                for i, (a, b) in enumerate(terms):
                    mm = pe.matmul(dst, a, b, start=i == 0, stop=i == len(terms) - 1)
            mm.then_inc(go_mm, 1)

        for a in range(ATT_UNITS + 3):
            if a < ATT_UNITS:
                scores(a)
            if 2 <= a < ATT_UNITS + 2:
                transpose_probs(a - 2)
            if a < TILES:
                hgrn_out(a)
            if a >= 3:
                values(a - 3)

        def transpose_mix(t):
            pe.wait_ge(mix_rdy, t + 1)
            if t == 0:
                pe.wait_ge(pt_ev, ATT_UNITS)
            if t == 1:
                pe.wait_ge(ao_ev, TILES)
            if t >= 2:
                pe.wait_ge(mtl_done, t - 1)
            for k in range(KT):
                mm = pe.transpose(pair[2 + t % 2][:, tile(k)], mixed[:, t, tile(k)], ident[:, :])
            mm.then_inc(mt_mm, 1)

        transpose_mix(0)
        for t in range(TILES):
            if t + 1 < TILES:
                transpose_mix(t + 1)
            pe.wait_ge(mtl_done, t + 1)
            if t == 0:
                pe.wait_ge(ex_done, ATT_UNITS)
            if t >= 2:
                pe.wait_ge(h_sq, t - 1)
            for k in range(KT):
                if t == 0:
                    pe.wait_ge(wol_done, k + 1)
                for half in range(2):
                    cols = slice(half * 512, (half + 1) * 512)
                    mm = split_mm(pair[t % 2][:, cols], mth[t % 2][:, k, :], mtl[t % 2][:, k, :],
                                  woh[:, k, cols], wol[:, k, cols], k == 0, k == KT - 1)
            mm.then_inc(wo_mm, 1)

        pe.wait_ge(norm2_in, 32)
        pe.wait_ge(wo_mm, TILES)
        pe.sem_inc(used, SPLIT)
        for t in range(TILES + 2):
            if t < TILES:
                pe.wait_ge(xt_done, t + 1)
                if t >= 2:
                    pe.wait_ge(xtt_ev, t - 1)
                for k in range(KT):
                    mm = pe.transpose(pair[2 + t % 2][:, tile(k)], mixed[:, t, tile(k)], ident[:, :])
                mm.then_inc(xtt_mm, 1)
            if 1 <= t <= TILES:
                pe.wait_ge(xtt_ev, t)
                if t == 1:
                    pe.wait_ge(h_sq, TILES)
                for k in range(KT):
                    mm = pe.matmul(logits_bank(t - 1), rw_sb[:, k, :], xtt[(t - 1) % 2][:, k, :],
                                   start=k == 0, stop=k == KT - 1)
                mm.then_inc(lg_mm, 1)
            if t >= 2:
                pe.wait_ge(lg_ev, t - 1)
                pe.transpose(PB[:, 512 + (t - 2) * EXPERTS:512 + (t - 1) * EXPERTS], lg_t[:, tile(t - 2)],
                             ident[0:EXPERTS, 0:EXPERTS]).then_inc(lg_done, 1)
        pe.wait_ge(rt_v, 8)
        for j in range(4):
            mm = pe.transpose(PB[0:48, tile(j)], aff[:, j, :], ident[:, :])
        mm.then_inc(rt_t, 1)
        pe.wait_ge(top_v, 3 * (CAP_S // 8) + 7)
        pe.transpose(PC[0:SLOTS, 0:48], slot_token[:, :], ident[0:48, 0:48])
        pe.transpose(PC[0:SLOTS, 64:112], slot_gate[:, :], ident[0:48, 0:48]).then_inc(rt_t, 1)

        H1, H3 = (PA[:, 0:512], PA[:, 512:1024]), (PB[:, 0:512], PB[:, 512:1024])
        TB = (PC[:, 0:512], PC[:, 512:1024])

        def transpose_rows(j, value):
            if j == 0:
                pe.wait_ge(xe_in, value)
            for k in range(4):
                mm = pe.transpose(TB[j][:, k * SLOTS:(k + 1) * SLOTS], xe[:, tile(4 * j + k)],
                                  ident[0:SLOTS, 0:SLOTS])
            mm.then_inc(t_mm, 1)

        pe.wait_ge(route_done, 2)
        for j in range(2):
            transpose_rows(j, 16)

        def expert(e, last):
            def hid_tiles(fc):
                return range(TILES_AFTER[fc - 1] if fc else 0, TILES_AFTER[fc])

            for c in range(CHUNKS):
                pe.wait_ge(cl_done, e * CHUNKS + (c + 1))
                hi, lo = chunk_view(ch[c % SPLIT], c), chunk_view(cl[c % SPLIT], c)
                if c < 2 * NFC:
                    fc = c // 2
                    if c == 0:
                        pe.wait_ge(tl_done, e * T_PER_EXPERT + 2)
                    if c % 2 == 0:
                        pe.wait_ge(hid_done, e * NFC + (fc + 1))
                    dst = (H1, H3)[c % 2][fc % 2][0:SLOTS, 0:FC]
                    for k in range(KT):
                        mm = split_mm(dst, xeh[:, k, :], xel[:, k, :], hi[:, k, :], lo[:, k, :],
                                      k == 0, k == KT - 1)
                else:
                    j = c - 2 * NFC
                    if j == 0:
                        pe.wait_ge(y_ev, e + 1)
                    if j == len(W2_KT) - 2:
                        pe.wait_ge(tl_done, e * T_PER_EXPERT + (2 + NFC))
                    elif j == 0:
                        pe.wait_ge(tl_done, e * T_PER_EXPERT + (1 + NFC))
                    for k in range(W2_KT[j]):
                        kk = W2_AT[j] + k
                        for half in range(2):
                            cols = slice(half * 512, (half + 1) * 512)
                            mm = split_mm(PD[0:SLOTS, cols], hid_h[:, kk, :], hid_l[:, kk, :],
                                          hi[:, k, cols], lo[:, k, cols], kk == 0, kk == FT - 1)
                mm.then_inc(used, 1)
                if c >= 2 and c % 2 == 0 and c // 2 - 1 < NFC:
                    fc = c // 2 - 1
                    pe.wait_ge(hid_done, e * NFC + (fc + 3))
                    pe.wait_ge(tl_done, e * T_PER_EXPERT + (1 + fc))
                    for i, k in enumerate(hid_tiles(fc)):
                        mm = pe.transpose(TB[fc % 2][:, i * SLOTS:(i + 1) * SLOTS], hid[:, tile(k)],
                                          ident[0:SLOTS, 0:SLOTS])
                    mm.then_inc(t_mm, 1)
                if not last and c in (2 * NFC + 2, 2 * NFC + 3):
                    j = c - 2 * NFC - 2
                    pe.wait_ge(tl_done, e * T_PER_EXPERT + (1 + NFC + j))
                    transpose_rows(j, e * 16 + 32)

        with pe.Fori(0, EXPERTS - 1) as e:
            expert(e, False)
        expert(EXPERTS - 1, True)

    @block.scalar
    def _(act):
        def high_part(hc):
            act.wait_ge(w_in_sem[hc % 2], 16 * (hc // 2 + 1))
            if hc >= 2:
                act.wait_ge(*split_slot_free(hc))
            act.activation(wh[hc % 2][:, :, :], raw_w[hc % 2][:, :, :], ACT.Copy).then_inc(wh_done, 1)

        for t in range(TILES):
            act.wait_ge(x_tile_in[t], 16)
            if t >= 2:
                act.wait_ge(x_sq, t - 1)
            act.activation(pair[t % 2][:, :], x_in[:, t, :], ACT.Square, accum_out=stat1[:, t:t + 1]).then_inc(x_sq, 1)
        act.wait_ge(setup_v, 1)
        act.activation(rstd1[:, :], stat1[:, :], ACT.Sqrt).then_inc(x_std, 1)
        high_part(0)
        for t in range(TILES):
            act.wait_ge(x_t, t + 1)
            act.activation(xh[:, :, tile(t)], pair[2 + t % 2][:, :].rearrange("p (k n) -> p k n", k=KT),
                           ACT.Copy).then_inc(xh_done, 1)
        high_part(1)
        act.wait_ge(setup_v, 6)
        act.activation(lam_s[:, :], lam_s[:, :], ACT.Exp).then_inc(setup_a, 1)
        act.activation(lb_raw[:, :, :, :], lb_raw[:, :, :, :], ACT.Exp).then_inc(setup_a, 1)
        for u in range(FM_UNITS):
            if u % 2 == 0 and u >= 2:
                high_part(u // 2 + 1)
            act.wait_ge(fm_mm, u + 1)
            if u < HEADS:
                if u >= 2:
                    act.wait_ge(q_done, u - 1)
                dst = e2[u % 2][:, :]
            else:
                dst = gate[:, u - HEADS, :]
            if u == 0:
                act.wait_ge(x_t, TILES)
            act.activation(dst[:, PROMPT:T], pair[u % 2][:, 0:SAMPLE], ACT.Sigmoid)
            act.activation(dst[:, 0:PROMPT], pair[u % 2][:, 512:512 + PROMPT], ACT.Sigmoid).then_inc(fm_act, 1)
        high_part(FM_PIECES + 1)
        for hd in range(8):
            act.wait_ge(k_done, hd + 1)
            act.activation(gate[:, hd, :], gate[:, hd, :], ACT.Ln).then_inc(ln_done, 1)

        def evacuate_projection(n):
            act.wait_ge(tm_mm, n + 1)
            if n >= STAGES:
                act.wait_ge(stage_out[n % STAGES], 16 * (n // STAGES))
            src = PC[:, (n % 2) * 512:(n % 2) * 512 + HC]
            piece = n // TILES
            normed = 4 <= piece < 8
            ins = act.activation(stage[n % STAGES][:, :], src, ACT.Copy).then_inc(stage_full, 1)
            if normed:
                m = n - 4 * TILES
                if m >= 2:
                    act.wait_ge(sq_used, m - 1)
                act.activation(sq[m % 2][:, :], src, ACT.Square).then_inc(sq_full, 1)
                act.wait_ge(sq_full, m + 1)
            act.wait_ge(stage_full, n + 1)
            act.sem_inc(tm_ev, 1)

        def decays(h, d):
            hd = d * 4 + h
            if h >= 1:
                act.wait_ge(fac, 4 * h)
            for t in range(TILES):
                act.activation(e2[d][:, tile(t)], gate[:, hd, tile(t)], ACT.Exp,
                               bias=btot[:, hd, t:t + 1], scale=-1.0).then_inc(e2_done, 1)
            act.wait_ge(e2_done, TILES * (2 * h + d + 1))
            act.activation(gate[:, hd, :], gate[:, hd, :], ACT.Exp).then_inc(e_done, 1)

        for n in range(LU_AT[-1] + 4):
            if n >= TILES and n % TILES == 0 and FM_PIECES + 1 + n // TILES < PIECES:
                high_part(FM_PIECES + 1 + n // TILES)
            if n < TM_UNITS:
                evacuate_projection(n)
            if n == LAG:
                act.wait_ge(scan_v, 24)
                act.activation(chunk_decay[:, :, :], btot[:, :, :], ACT.Exp).then_inc(decay_done, 1)
            for d in range(2):
                last = n - 1 - 2 * d
                if last in LU_AT and LU_AT.index(last) % PER_HEAD == NL:
                    decays(LU_AT.index(last) // PER_HEAD, d)
            i = LU_AT.index(n) if n in LU_AT else None
            if i is not None and level_of(i)[1] is not None:
                lv = levels_to(i)
                act.wait_ge(x_sub, lv)
                act.activation(xl[(lv - 1) % 3][:, :, :], xl[(lv - 1) % 3][:, :, :], ACT.Exp).then_inc(x_exp, 1)
        act.wait_ge(qk_v, 1)
        act.activation(qk_rstd[:, :, :], qk_ss[:, :, :], ACT.Sqrt).then_inc(qk_std, 1)
        for w in range(len(STATE_UNITS)):
            act.wait_ge(kd_t, w + 1)
            if w >= 2:
                act.wait_ge(u_mm, w - 1)
            act.activation(kdec_tm[w % 2][:, :], PC[:, (w % 2) * 512:(w % 2 + 1) * 512], ACT.Copy).then_inc(kd_ev, 1)
            if w < TILES:
                act.wait_ge(qk_t, w + 1)
                act.activation(qt[:, :, tile(w)], pair[w % 2][:, 0:512].rearrange("p (h n) -> p h n", h=HEADS), ACT.Copy)
                act.activation(kt_[:, :, tile(w)], pair[w % 2][:, 512:1024].rearrange("p (h n) -> p h n", h=HEADS),
                               ACT.Copy).then_inc(qk_ev, 1)

        def evac_probs(a):
            n = KEY_TILES[a // HEADS] * P
            act.wait_ge(pt_mm, a + 1)
            if a >= 2:
                act.wait_ge(pv_mm, a - 1)
            act.activation(probs_t[a % 2][:, 0:n], PC[:, (a % 2) * 512:(a % 2) * 512 + n], ACT.Copy).then_inc(pt_ev, 1)

        def w_out_high(k):
            act.wait_ge(wo_in[k % 2], 16 * (k // 2 + 1))
            act.activation(woh[:, k, :], wo_raw[k % 2][:, :], ACT.Copy).then_inc(woh_done, 1)

        def gate_silu(t):
            act.wait_ge(hg_in[t % 2], 16 * (t // 2 + 1))
            act.activation(hg[t % 2][:, :], hg[t % 2][:, :], ACT.Silu).then_inc(hg_act, 1)

        for a in range(ATT_UNITS + 4):
            if 2 <= a < ATT_UNITS + 2:
                evac_probs(a - 2)
            if a < ATT_UNITS:
                n = KEY_TILES[a // HEADS] * P
                act.wait_ge(mx_done, a + 1)
                if a >= PROBS:
                    act.wait_ge(pt_mm, a - PROBS + 1)
                for c in range(2):
                    ins = act.activation(probs[a % PROBS][:, c, 0:n], scores_of(a)[:, c * 512:c * 512 + n], ACT.Exp,
                                         bias=neg_max[:, a, c:c + 1], scale=QK_DIM ** -0.5,
                                         accum_out=exp_sum[:, a, c:c + 1])
                ins.then_inc(ex_done, 1)
            if a < TILES:
                act.wait_ge(go_mm, a + 1)
                act.activation(mixed[:, a, 0:512], PD[:, 512:1024], ACT.Copy).then_inc(go_ev, 1)
            if (a - WO_AT) % 2 == 0 and 0 <= (a - WO_AT) // 2 < KT:
                w_out_high((a - WO_AT) // 2)
            if a == WO_AT + 3:
                gate_silu(0)
                gate_silu(1)
            if a >= HEADS + 3 and (a - 3) % HEADS == 0:
                t = (a - 3) // HEADS - 1
                act.wait_ge(pv_mm, HEADS * (t + 1))
                act.activation(mixed[:, t, 512:1024], PD[:, 0:512], ACT.Copy).then_inc(ao_ev, 1)
                if t >= 1:
                    act.wait_ge(o_red, t)
                act.wait_ge(ao_ev, t + 1)
                act.wait_ge(go_ev, t + 1)
                act.activation(sq_o[:, :], mixed[:, t, :], ACT.Square).then_inc(o_sq, 1)
            if a == NORM_AT:
                act.wait_ge(o_v, 1)
                act.activation(head_rstd[:, 0:4, :], head_ss[:, 0:4, :], ACT.Sqrt).then_inc(o_std, 1)
        act.wait_ge(o_v, 3)
        act.activation(head_rstd[:, 4:6, :], head_ss[:, 4:6, :], ACT.Sqrt).then_inc(o_std, 1)

        def mix_high(t):
            act.wait_ge(mt_mm, t + 1)
            if t >= 2:
                act.wait_ge(wo_mm, t - 1)
            act.activation(mth[t % 2][:, :, :], pair[2 + t % 2][:, :].rearrange("p (k n) -> p k n", k=KT),
                           ACT.Copy).then_inc(mth_done, 1)

        mix_high(0)
        for t in range(TILES):
            if t + 1 < TILES:
                mix_high(t + 1)
            if t + 2 < TILES:
                gate_silu(t + 2)
            act.wait_ge(h_done, t + 1)
            act.activation(pair[t % 2][:, :], mixed[:, t, :], ACT.Square, accum_out=stat2[:, t:t + 1]).then_inc(h_sq, 1)
            if t == 4:
                act.wait_ge(h_v, 1)
                act.activation(rstd2[:, 0:4], stat2[:, 0:4], ACT.Sqrt).then_inc(h_std, 1)
        def logits(t):
            act.wait_ge(lg_mm, t + 1)
            act.activation(lg_t[:, tile(t)], logits_bank(t), ACT.Copy).then_inc(lg_ev, 1)

        for t in range(TILES):
            if t == 2:
                act.wait_ge(h_v, 3)
                act.activation(rstd2[:, 4:6], stat2[:, 4:6], ACT.Sqrt).then_inc(h_std, 1)
            act.wait_ge(xtt_mm, t + 1)
            if t >= 2:
                act.wait_ge(lg_mm, t - 1)
            act.activation(xtt[t % 2][:, :, :], pair[2 + t % 2][:, :].rearrange("p (k n) -> p k n", k=KT),
                           ACT.Copy).then_inc(xtt_ev, 1)
            if t >= 1:
                logits(t - 1)
        logits(TILES - 1)
        act.wait_ge(rt_v, 3)
        act.activation(lexp[:, :, :], logit[:, :, :], ACT.Exp).then_inc(rt_exp, 1)

        H1 = (PA[:, 0:512], PA[:, 512:1024])
        TB = (PC[:, 0:512], PC[:, 512:1024])

        def rows_high(j, value):
            act.wait_ge(t_mm, value)
            act.activation(xeh[:, 4 * j:4 * j + 4, :], TB[j][:, 0:4 * SLOTS].rearrange("p (k n) -> p k n", k=4),
                           ACT.Copy).then_inc(th_done, 1)

        def chunk_high(e, c):
            act.wait_ge(raw_in[c % RING], e * (16 * CHUNKS // RING) + 16 * (c // RING + 1))
            act.wait_ge(used, e * CHUNKS + (c + 1))
            n = chunk_size(c % CHUNKS)
            act.activation(ch[c % SPLIT][:, 0:n], ring[c % RING][:, 0:n], ACT.Copy).then_inc(ch_done, 1)

        def expert(e, last):
            for cc in range(2, CHUNKS + 2):
                if cc < CHUNKS or not last:
                    chunk_high(e, cc)
                c = cc - 2
                if c % 2 == 0 and c < 2 * NFC:
                    fc = c // 2
                    act.wait_ge(used, e * CHUNKS + (c + 1 + SPLIT))
                    act.activation(silu[fc % 2][:, :], H1[fc % 2][0:SLOTS, 0:FC], ACT.Silu).then_inc(silu_done, 1)
                if c >= 2 and c % 2 == 0 and c // 2 - 1 < NFC:
                    fc = c // 2 - 1
                    k0, k1 = (TILES_AFTER[fc - 1] if fc else 0), TILES_AFTER[fc]
                    act.wait_ge(t_mm, e * T_PER_EXPERT + (3 + fc))
                    act.activation(hid_h[:, k0:k1, :],
                                   TB[fc % 2][:, 0:(k1 - k0) * SLOTS].rearrange("p (k n) -> p k n", k=k1 - k0),
                                   ACT.Copy).then_inc(th_done, 1)
                if not last and c in (2 * NFC + 2, 2 * NFC + 3):
                    j = c - 2 * NFC - 2
                    rows_high(j, e * T_PER_EXPERT + (3 + NFC + j))
                if c == CHUNKS - 1:
                    act.wait_ge(used, e * CHUNKS + (CHUNKS + SPLIT))
                    act.wait_ge(y_free, e + 1)
                    for half in range(2):
                        cols = slice(half * 512, (half + 1) * 512)
                        ins = act.activation(y_sb[:, cols], PD[0:SLOTS, cols], ACT.Copy, scale=gates[:, bass.ds(e, 1)])
                    ins.then_inc(y_ev, 1)

        chunk_high(0, 0)
        chunk_high(0, 1)
        act.wait_ge(route_done, 2)
        rows_high(0, 1)
        rows_high(1, 2)
        act.sem_inc(y_ev, 1)
        with act.Fori(0, EXPERTS - 1) as e:
            expert(e, False)
        expert(EXPERTS - 1, True)

    @block.vector
    def _(dve):
        def low_part(hc):
            dve.wait_ge(wh_done, hc + 1)
            dve.tensor_tensor(wl[hc % 2][:, :, :], raw_w[hc % 2][:, :, :], wh[hc % 2][:, :, :].bitcast(F32),
                              ALU.subtract).then_inc(wl_done, 1)

        dve.wait_ge(x_sq, TILES)
        dve.tensor_scalar(stat1[:, :], stat1[:, :], 1.0 / D, EPS, ALU.mult, ALU.add).then_inc(setup_v, 1)
        dve.wait_ge(x_std, 1)
        dve.reciprocal(rstd1[:, :], rstd1[:, :]).then_inc(x_rstd, 1)
        dve.wait_ge(x_rstd, 1)
        dve.wait_ge(consts_in, 16 * NCONST)
        for t in range(TILES):
            dve.scalar_tensor_tensor(out=x_scaled[:, t, :], in0=x_in[:, t, :], scalar=rstd1[:, t:t + 1],
                                     in1=norm1_bc[:, :], op0=ALU.mult, op1=ALU.mult).then_inc(xs_ready, 1)
        low_part(0)
        for i in range(2):
            dve.tensor_tensor(lam_p[:, i, :], lam4[:, 2 * i, :], lam4[:, 2 * i + 1, :], ALU.mult).then_inc(setup_v, 1)
        dve.wait_ge(lb_in, 64)
        dve.tensor_tensor(lb_max[:, :, :], lb_raw[:, :, 0, :], lb_raw[:, :, 1, :], ALU.max).then_inc(setup_v, 1)
        dve.wait_ge(setup_v, 4)
        dve.tensor_reduce(lam_s[:, :], lam_p[:, :, :], AX.X, ALU.add).then_inc(setup_v, 1)
        for r in range(2):
            ins = dve.tensor_tensor(lb_raw[:, :, r, :], lb_raw[:, :, r, :], lb_max[:, :, :], ALU.subtract)
        ins.then_inc(setup_v, 1)
        for t in range(TILES):
            dve.wait_ge(xh_done, t + 1)
            dve.tensor_tensor(xlo[:, :, tile(t)], pair[2 + t % 2][:, :].rearrange("p (k n) -> p k n", k=KT),
                              xh[:, :, tile(t)].bitcast(F32), ALU.subtract).then_inc(xl_done, 1)
        low_part(1)
        dve.wait_ge(setup_a, 2)
        dve.tensor_tensor(neg_lam[:, :], lam_s[:, 1:2], lam_s[:, 0:1], ALU.subtract).then_inc(setup_v, 1)
        dve.tensor_tensor(lb_max[:, :, :], lb_raw[:, :, 0, :], lb_raw[:, :, 1, :], ALU.add).then_inc(setup_v, 1)
        dve.wait_ge(setup_v, 8)
        dve.tensor_scalar(neg_lam[:, :], neg_lam[:, :], -LAM_INIT, None, ALU.add).then_inc(setup_v, 1)
        dve.reciprocal(lb_max[:, :, :], lb_max[:, :, :]).then_inc(setup_v, 1)
        dve.tensor_scalar(norm_w[:, 1, :], norm_w[:, 1, :], 1.0 - LAM_INIT, None, ALU.mult).then_inc(setup_v, 1)
        dve.wait_ge(setup_v, 11)
        dve.tensor_tensor(lb[:, :, :], lb_raw[:, :, 0, :], lb_max[:, :, :], ALU.mult).then_inc(setup_v, 1)
        dve.wait_ge(setup_v, 12)
        dve.tensor_scalar(one_minus_lb[:, :, :], lb[:, :, :], -1.0, 1.0, ALU.mult, ALU.add).then_inc(setup_v, 1)
        dve.wait_ge(setup_v, 13)
        dve.wait_ge(x_t, TILES)
        for u in range(FM_UNITS):
            if u % 2 == 0 and u >= 2:
                low_part(u // 2 + 1)
            dve.wait_ge(fm_act, u + 1)
            if u < HEADS:
                for d0, d1, p0 in ((PROMPT, T, 0), (0, PROMPT, 512)):
                    ins = dve.scalar_tensor_tensor(out=q_fm[:, u, d0:d1], in0=pair[u % 2][:, p0:p0 + d1 - d0],
                                                   scalar=float(P) ** -0.5, in1=e2[u % 2][:, d0:d1],
                                                   op0=ALU.mult, op1=ALU.mult)
                ins.then_inc(q_done, 1)
            else:
                hd = u - HEADS
                d, h = divmod(hd, HEADS)
                dve.tensor_scalar(gate[:, hd, :], gate[:, hd, :], one_minus_lb[:, d, h:h + 1], lb[:, d, h:h + 1],
                                  ALU.mult, ALU.add).then_inc(f_done, 1)
                dve.wait_ge(f_done, hd + 1)
                dve.tensor_scalar(keys[:, hd, :], gate[:, hd, :], -1.0, 1.0, ALU.mult, ALU.add).then_inc(k_done, 1)
        low_part(FM_PIECES + 1)
        dve.memset(restart[:, :], 1.0).then_inc(scan_v, 1)
        dve.wait_ge(scan_v, 1)
        starts = restart[:, :].rearrange("p (t n) -> p t n", n=P)
        dve.memset(starts[:, :, 0:1], 0.0).then_inc(scan_v, 1)
        dve.wait_ge(scan_v, 2)
        done = 2
        for hd in range(8):
            dve.wait_ge(ln_done, hd + 1)
            dst = gate[:, hd, :] if hd < 4 else lev_tmp[:, :]
            if hd > 4:
                dve.wait_ge(scan_v, done)
            dve.tensor_tensor_scan(dst, restart[:, :], gate[:, hd, :], 0.0, ALU.mult, ALU.add).then_inc(scan_v, 1)
            done += 1
            dve.wait_ge(scan_v, done)
            ends = dst.rearrange("p (t n) -> p t n", n=P)
            dve.tensor_copy(btot[:, hd, :].unsqueeze(2), ends[:, :, P - 1:P]).then_inc(scan_v, 1)
            done += 1
            if hd >= 4:
                dve.tensor_tensor(gate[:, hd, :], lev_tmp[:, :], gate[:, hd, :], ALU.subtract).then_inc(scan_v, 1)
                done += 1
        done += 2
        assert done == 24, done
        dve.sem_inc(scan_v, 2)
        dve.wait_ge(scan_v, done)

        def halves(a, m):
            v = a.rearrange("p (b s m) -> p b s m", s=2, m=m)
            return v[:, :, 0, :], v[:, :, 1, :]

        def level_buffer(i):
            m = LEVELS[level_of(i)[1]]
            lv = xl[(levels_to(i) - 1) % 3]
            return m, lv, halves(lv[:, 0, :], m), halves(lv[:, 1, :], m)

        def subtract(i):
            h, level = level_of(i)
            if level is None:
                return
            m, _, (key0, key1), (query0, query1) = level_buffer(i)
            if levels_to(i) > 3:
                last = next(j for j in range(i) if levels_to(j) == levels_to(i) - 3 and level_of(j)[1] is not None)
                dve.wait_ge(lu_mm, last + 1)
            for d, first, second in ((0, key0, query1), (1, query0, key1)):
                b0, b1 = halves(gate[:, d * 4 + h, :], m)
                mid = b0[:, :, m - 1:m].to_broadcast([P, T // (2 * m), m])
                dve.tensor_tensor(first, mid, b0, ALU.subtract)
                ins = dve.tensor_tensor(second, b1, mid, ALU.subtract)
            ins.then_inc(x_sub, 1)

        def multiply(i):
            h, level = level_of(i)
            if level is None:
                return
            m, lv, (key0, key1), _ = level_buffer(i)
            dve.wait_ge(x_exp, levels_to(i))
            dve.tensor_tensor(key0, key0, halves(keys[:, h, :], m)[0], ALU.mult)
            dve.tensor_tensor(key1, key1, halves(keys[:, 4 + h, :], m)[1], ALU.mult)
            dve.tensor_tensor(lv[:, 1, :], lv[:, 1, :], q_fm[:, h, :], ALU.mult).then_inc(x_rdy, 1)

        def merge(i):
            h, level = level_of(i)
            dve.wait_ge(lu_mm, i + 1)
            if level is not None:
                dve.wait_ge(lu_ev, i)
            for g in range(2):
                dst = att_t[:, h, g * 384:(g + 1) * 384].rearrange("p (t n) -> p t n", n=P)
                src = pair[i % 2][:, g * 512:g * 512 + 384].rearrange("p (t n) -> p t n", n=P)
                if level is None:
                    ins = dve.tensor_tensor(dst, src, ident[:, :].unsqueeze(1).to_broadcast([P, 3, P]), ALU.mult)
                else:
                    mask = masks[:, level, :].unsqueeze(1).to_broadcast([P, 3, P])
                    ins = dve.copy_predicated(dst, mask, src)
            ins.then_inc(lu_ev, 1)

        def projection_squares(n):
            m = n - 4 * TILES
            piece, t = divmod(m, TILES)
            dve.wait_ge(sq_full, m + 1)
            dve.tensor_reduce(qk_ss[:, t, piece * 4:piece * 4 + 4],
                              sq[m % 2][:, :].rearrange("p (g n) -> p g n", n=QK_DIM), AX.X, ALU.add).then_inc(sq_used, 1)

        dve.wait_ge(masks_in, 16)
        dve.tensor_copy(masks[:, :, :], masks_f[:, :, :]).then_inc(masks_done, 1)
        dve.wait_ge(masks_done, 1)
        for n in range(LU_AT[-1] + 4):
            if n in LU_AT:
                subtract(LU_AT.index(n))
            if n >= TILES and n % TILES == 0 and FM_PIECES + 1 + n // TILES < PIECES:
                low_part(FM_PIECES + 1 + n // TILES)
            if n - 1 in LU_AT:
                multiply(LU_AT.index(n - 1))
            if n - 3 in LU_AT:
                merge(LU_AT.index(n - 3))
            if 4 * TILES <= n - 1 < 8 * TILES:
                projection_squares(n - 1)
        dve.wait_ge(sq_used, 4 * TILES)
        dve.tensor_scalar(qk_ss[:, :, :], qk_ss[:, :, :], 1.0 / QK_DIM, EPS, ALU.mult, ALU.add).then_inc(qk_v, 1)
        dve.wait_ge(qk_std, 1)
        dve.reciprocal(qk_rstd[:, :, :], qk_rstd[:, :, :]).then_inc(qk_v, 1)

        def state(w):
            d, t = STATE_UNITS[w]
            before = (d, t - 1 if d == 0 else t + 1)
            dve.wait_ge(u_mm, w + 1)
            src = PD[:, (w % 2) * 512:(w % 2 + 1) * 512]
            if before not in STATE_UNITS:
                dve.tensor_copy(states[:, w, :], src).then_inc(s_done, 1)
                return
            old = STATE_UNITS.index(before)
            dve.wait_ge(s_done, old + 1)
            dve.wait_ge(decay_done, 1)
            for h in range(HEADS):
                ins = dve.scalar_tensor_tensor(out=states[:, w, tile(h)], in0=states[:, old, tile(h)],
                                               scalar=chunk_decay[:, d * 4 + h, t:t + 1], in1=src[:, tile(h)],
                                               op0=ALU.mult, op1=ALU.add)
            ins.then_inc(s_done, 1)

        qv = 2
        for w in range(len(STATE_UNITS) + 1):
            if w < TILES:
                t = w
                dve.wait_ge(qk_v, qv)
                dve.wait_ge(qk_in[t % 2], 16 * (t // 2 + 1))
                g = qk[t % 2][:, :].rearrange("p (g n) -> p g n", n=QK_DIM)
                dve.tensor_tensor(g, g, qk_rstd[:, t, :].unsqueeze(2).to_broadcast([P, 16, QK_DIM]), ALU.mult).then_inc(qk_v, 1)
                dve.wait_ge(qk_v, qv + 1)
                g4 = qk[t % 2][:, :].rearrange("p (s g n) -> p s g n", s=2, n=QK_DIM)
                dve.tensor_tensor(g4, g4, qk_w[:, :, :].unsqueeze(2).to_broadcast([P, 2, 8, QK_DIM]), ALU.mult).then_inc(qk_v, 1)
                dve.wait_ge(qk_v, qv + 2)
                x1, x2 = g[:, :, 0:8], g[:, :, 8:16]
                c_b = cos[:, t, :].unsqueeze(1).to_broadcast([P, 16, 8])
                s_b = sin[:, t, :].unsqueeze(1).to_broadcast([P, 16, 8])
                for r, (a, b) in enumerate(((x1, c_b), (x2, s_b), (x2, c_b), (x1, s_b))):
                    ins = dve.tensor_tensor(rope_t[:, r, :, :], a, b, ALU.mult)
                ins.then_inc(qk_v, 1)
                dve.wait_ge(qk_v, qv + 3)
                dve.tensor_tensor(x1, rope_t[:, 0, :, :], rope_t[:, 1, :, :], ALU.subtract)
                dve.tensor_tensor(x2, rope_t[:, 2, :, :], rope_t[:, 3, :, :], ALU.add).then_inc(qk_rdy, 1)
                qv += 3
            if w >= 1:
                state(w - 1)

        def score_max(a):
            n = KEY_TILES[a // HEADS] * P
            dve.wait_ge(sc_mm, a + 1)
            dve.tensor_reduce(neg_max[:, a, :], scores_of(a)[:, :].rearrange("p (c n) -> p c n", c=2)[:, :, 0:n],
                              AX.X, ALU.max, negate=True).then_inc(mx_v, 1)
            dve.wait_ge(mx_v, a + 1)
            dve.tensor_scalar(neg_max[:, a, :], neg_max[:, a, :], QK_DIM ** -0.5, None, ALU.mult).then_inc(mx_done, 1)

        def difference(a):
            n = KEY_TILES[a // HEADS] * P
            dve.wait_ge(ex_done, a + 1)
            dve.reciprocal(exp_r[:, a, :], exp_sum[:, a, :]).then_inc(pd_v, 1)
            dve.wait_ge(pd_v, 3 * a + 1)
            dve.tensor_tensor(exp_r[:, a, 1:2], exp_r[:, a, 1:2], neg_lam[:, :], ALU.mult).then_inc(pd_v, 1)
            dve.tensor_scalar(probs[a % PROBS][:, 0, 0:n], probs[a % PROBS][:, 0, 0:n], exp_r[:, a, 0:1], None, ALU.mult).then_inc(pd_v, 1)
            dve.wait_ge(pd_v, 3 * a + 3)
            dve.scalar_tensor_tensor(out=probs[a % PROBS][:, 0, 0:n], in0=probs[a % PROBS][:, 1, 0:n], scalar=exp_r[:, a, 1:2],
                                     in1=probs[a % PROBS][:, 0, 0:n], op0=ALU.mult, op1=ALU.add).then_inc(pd_rdy, 1)

        def mean_squares(tiles, red):
            dve.wait_ge(o_red, red)
            dve.tensor_scalar(head_ss[:, tiles, :], head_ss[:, tiles, :], 1.0 / P, EPS, ALU.mult, ALU.add).then_inc(o_v, 1)

        def reciprocal_std(tiles, group):
            dve.wait_ge(o_std, group + 1)
            dve.reciprocal(head_rstd[:, tiles, :], head_rstd[:, tiles, :]).then_inc(o_v, 1)
            dve.wait_ge(o_v, 2 * group + 2)

        def mix(t):
            o = mixed[:, t, :].rearrange("p (g n) -> p g n", n=P)
            o4 = mixed[:, t, :].rearrange("p (s g n) -> p s g n", s=2, n=P)
            dve.tensor_tensor(o, o, head_rstd[:, t, :].unsqueeze(2).to_broadcast([P, 8, P]), ALU.mult).then_inc(mix_v, 1)
            dve.wait_ge(mix_v, 2 * t + 1)
            dve.tensor_tensor(o4, o4, norm_w[:, :, :].unsqueeze(2).to_broadcast([P, 2, 4, P]), ALU.mult).then_inc(mix_v, 1)
            dve.wait_ge(mix_v, 2 * t + 2)
            dve.wait_ge(hg_act, t + 1)
            dve.tensor_tensor(mixed[:, t, 0:512], mixed[:, t, 0:512], hg[t % 2][:, :], ALU.mult).then_inc(mix_rdy, 1)

        def mix_low(t):
            dve.wait_ge(mth_done, t + 1)
            dve.tensor_tensor(mtl[t % 2][:, :, :], pair[2 + t % 2][:, :].rearrange("p (k n) -> p k n", k=KT),
                              mth[t % 2][:, :, :].bitcast(F32), ALU.subtract).then_inc(mtl_done, 1)

        for a in range(ATT_UNITS + 4):
            if a < ATT_UNITS:
                score_max(a)
            if 1 <= a <= ATT_UNITS:
                difference(a - 1)
            if (a - WO_AT - 1) % 2 == 0 and 0 <= (a - WO_AT - 1) // 2 < KT:
                k = (a - WO_AT - 1) // 2
                dve.wait_ge(woh_done, k + 1)
                dve.tensor_tensor(wol[:, k, :], wo_raw[k % 2][:, :], woh[:, k, :].bitcast(F32), ALU.subtract).then_inc(wol_done, 1)
            if a >= HEADS + 3 and (a - 3) % HEADS == 0:
                t = (a - 3) // HEADS - 1
                dve.wait_ge(o_sq, t + 1)
                dve.tensor_reduce(head_ss[:, t, :], sq_o[:, :].rearrange("p (g n) -> p g n", n=P), AX.X, ALU.add).then_inc(o_red, 1)
            if a == NORM_AT:
                mean_squares(slice(0, 4), 4)
            if a == NORM_AT + 1:
                reciprocal_std(slice(0, 4), 0)
                mix(0)
            if a == NORM_AT + 2:
                mix(1)
        mean_squares(slice(4, 6), 6)
        mix_low(0)
        reciprocal_std(slice(4, 6), 1)
        for t in range(TILES):
            if t + 1 < TILES:
                mix_low(t + 1)
            if t + 2 < TILES:
                mix(t + 2)
            dve.wait_ge(wo_mm, t + 1)
            dve.wait_ge(xa_in[t % 2], 16 * (t // 2 + 1))
            dve.tensor_tensor(mixed[:, t, :], pair[t % 2][:, :], x_again[t % 2][:, :], ALU.add).then_inc(h_done, 1)
            if t == 4:
                dve.wait_ge(h_sq, 4)
                dve.tensor_scalar(stat2[:, 0:4], stat2[:, 0:4], 1.0 / D, EPS, ALU.mult, ALU.add).then_inc(h_v, 1)
                dve.wait_ge(h_std, 1)
                dve.reciprocal(rstd2[:, 0:4], rstd2[:, 0:4]).then_inc(h_v, 1)
                dve.wait_ge(h_v, 2)
        dve.wait_ge(norm2_in, 32)
        for t in range(TILES):
            if t == 2:
                dve.wait_ge(h_sq, TILES)
                dve.tensor_scalar(stat2[:, 4:6], stat2[:, 4:6], 1.0 / D, EPS, ALU.mult, ALU.add).then_inc(h_v, 1)
            if t == 4:
                dve.wait_ge(h_std, 2)
                dve.reciprocal(rstd2[:, 4:6], rstd2[:, 4:6]).then_inc(h_v, 1)
                dve.wait_ge(h_v, 4)
            dve.wait_ge(h_out[t], 16)
            dve.scalar_tensor_tensor(out=mixed[:, t, :], in0=mixed[:, t, :], scalar=rstd2[:, t:t + 1],
                                     in1=norm2_bc[:, :], op0=ALU.mult, op1=ALU.mult).then_inc(xt_done, 1)
        dve.wait_ge(lg_done, TILES)
        lg = PB[:, 512:512 + TILES * EXPERTS].rearrange("p (t e) -> p t e", e=EXPERTS)
        dve.tensor_reduce(lmax[:, :], lg, AX.X, ALU.max).then_inc(rt_v, 1)
        dve.memset(aff[:, :, :], -1.0).then_inc(rt_v, 1)
        dve.wait_ge(rt_v, 2)
        dve.tensor_tensor(logit[:, :, :], lg, lmax[:, :].unsqueeze(2).to_broadcast([P, TILES, EXPERTS]), ALU.subtract).then_inc(rt_v, 1)
        dve.wait_ge(rt_exp, 1)
        dve.tensor_reduce(lsum[:, :], lexp[:, :, :], AX.X, ALU.add).then_inc(rt_v, 1)
        dve.wait_ge(rt_v, 4)
        dve.reciprocal(lsum[:, :], lsum[:, :]).then_inc(rt_v, 1)
        dve.wait_ge(rt_v, 5)
        for at, t0, n in ((0, PROMPT_TILES, 4), (32, 0, PROMPT_TILES)):
            dve.tensor_tensor(aff[:, 0:n, at:at + EXPERTS], lexp[:, t0:t0 + n, :],
                              lsum[:, t0:t0 + n].unsqueeze(2).to_broadcast([P, n, EXPERTS]), ALU.mult).then_inc(rt_v, 1)
        dve.memset(slot_gate[:, :], 0.0).then_inc(rt_v, 1)
        dve.memset(slot_token[:, :], 0.0).then_inc(top_v, 1)
        dve.wait_ge(rt_t, 1)
        dve.tensor_copy(aff_t[0][:, :], PB[0:48, 0:SAMPLE]).then_inc(top_v, 1)
        n = 2
        for r in range(CAP_S // 8):
            dve.wait_ge(top_v, n)
            cols = slice(8 * r, 8 * r + 8)
            dve.max(top[:, cols], aff_t[r % 2][:, :]).then_inc(top_v, 1)
            dve.wait_ge(top_v, n + 1)
            dve.max_index(top_i[:, cols], top[:, cols], aff_t[r % 2][:, :]).then_inc(top_v, 1)
            dve.match_replace(aff_t[(r + 1) % 2][:, :], top[:, cols], aff_t[r % 2][:, :], -2.0).then_inc(top_v, 1)
            n += 3
        dve.wait_ge(top_v, n)
        dve.tensor_copy(slot_gate[0:16, 0:CAP_S], top[0:16, :]).then_inc(top_v, 1)
        dve.tensor_copy(slot_gate[32:48, CAP_S:SLOTS], top[32:48, 0:CAP_P]).then_inc(top_v, 1)
        dve.tensor_copy(slot_token[0:16, 0:CAP_S], top_i[0:16, :]).then_inc(top_v, 1)
        dve.tensor_copy(slot_token[32:48, CAP_S:SLOTS], top_i[32:48, 0:CAP_P]).then_inc(top_v, 1)
        n += 4
        dve.wait_ge(top_v, n)
        dve.tensor_scalar(slot_token[0:16, 0:CAP_S], slot_token[0:16, 0:CAP_S], float(PROMPT), None, ALU.add).then_inc(top_v, 1)
        n += 1
        assert n == 3 * (CAP_S // 8) + 7
        dve.wait_ge(rt_t, 2)
        for o, dst in ((0, token), (64, gates)):
            dve.tensor_copy(dst[0:CAP_S, :], PC[0:CAP_S, o:o + 16])
            dve.tensor_copy(dst[CAP_S:SLOTS, :], PC[CAP_S:SLOTS, o + 32:o + 48]).then_inc(route_done, 1)

        H3 = (PB[:, 0:512], PB[:, 512:1024])
        TB = (PC[:, 0:512], PC[:, 512:1024])

        def rows_low(j, value):
            dve.wait_ge(th_done, value)
            dve.tensor_tensor(xel[:, 4 * j:4 * j + 4, :], TB[j][:, 0:4 * SLOTS].rearrange("p (k n) -> p k n", k=4),
                              xeh[:, 4 * j:4 * j + 4, :].bitcast(F32), ALU.subtract).then_inc(tl_done, 1)

        def chunk_low(e, c):
            n = chunk_size(c % CHUNKS)
            dve.wait_ge(ch_done, e * CHUNKS + (c + 1))
            dve.tensor_tensor(cl[c % SPLIT][:, 0:n], ring[c % RING][:, 0:n], ch[c % SPLIT][:, 0:n].bitcast(F32),
                              ALU.subtract).then_inc(cl_done, 1)

        def expert(e, last):
            for cc in range(2, CHUNKS + 2):
                if cc < CHUNKS or not last:
                    chunk_low(e, cc)
                c = cc - 2
                if c % 2 == 1 and c < 2 * NFC:
                    fc = c // 2
                    dve.wait_ge(silu_done, e * NFC + (fc + 1))
                    dve.wait_ge(used, e * CHUNKS + (c + 1 + SPLIT))
                    dve.tensor_tensor(hid[:, fc * FC:(fc + 1) * FC], H3[fc % 2][0:SLOTS, 0:FC], silu[fc % 2][:, :],
                                      ALU.mult).then_inc(hid_done, 1)
                if c >= 2 and c % 2 == 0 and c // 2 - 1 < NFC:
                    fc = c // 2 - 1
                    k0, k1 = (TILES_AFTER[fc - 1] if fc else 0), TILES_AFTER[fc]
                    dve.wait_ge(th_done, e * T_PER_EXPERT + (3 + fc))
                    dve.tensor_tensor(hid_l[:, k0:k1, :],
                                      TB[fc % 2][:, 0:(k1 - k0) * SLOTS].rearrange("p (k n) -> p k n", k=k1 - k0),
                                      hid_h[:, k0:k1, :].bitcast(F32), ALU.subtract).then_inc(tl_done, 1)
                if not last and c in (2 * NFC + 2, 2 * NFC + 3):
                    j = c - 2 * NFC - 2
                    rows_low(j, e * T_PER_EXPERT + (3 + NFC + j))

        dve.wait_ge(early_low, EARLY)
        dve.sem_inc(cl_done, EARLY)
        dve.sem_inc(hid_done, 2)
        rows_low(0, 1)
        rows_low(1, 2)
        with dve.Fori(0, EXPERTS - 1) as e:
            expert(e, False)
        expert(EXPERTS - 1, True)

    @block.gpsimd
    def _(pool):
        for h in range(HEADS):
            pool.wait_ge(lu_mm, PER_HEAD * (h + 1))
            for d in range(2):
                hd = d * 4 + h
                pool.wait_ge(e_done, 2 * h + d + 1)
                k_factor = e2[0][:, :] if d == 0 else gate[:, hd, :]
                q_factor = gate[:, hd, :] if d == 0 else e2[1][:, :]
                pool.tensor_tensor(keys[:, hd, :], keys[:, hd, :], k_factor, ALU.mult).then_inc(fac, 1)
                pool.wait_ge(fac, 4 * h + 2 * d + 1)
                pool.tensor_tensor(gate[:, hd, :], q_fm[:, h, :], q_factor, ALU.mult).then_inc(fac, 1)

        def gather(e):
            pool.indirect_dma_start(out=xe[:, :], out_offset=None, in_=xt_d,
                                    in_offset=bass.IndirectOffsetOnAxis(ap=token[:, e:e + 1], axis=0),
                                    bounds_check=T - 1).then_inc(xe_in, 16)

        for c in range(EARLY):
            n = chunk_size(c)
            pool.wait_ge(ch_done, c + 1)
            pool.tensor_tensor(cl[c][:, 0:n], ring[c][:, 0:n], ch[c][:, 0:n].bitcast(F32), ALU.subtract).then_inc(early_low, 1)
        pool.wait_ge(route_done, 2)
        pool.sem_inc(y_free, 1)
        pool.wait_ge(xt_out, 16 * TILES)
        gather(0)
        for e in range(EXPERTS):
            if e + 1 < EXPERTS:
                pool.wait_ge(t_mm, e * T_PER_EXPERT + 2)
                gather(e + 1)
            pool.wait_ge(y_ev, e + 2)
            pool.indirect_dma_start(out=out, out_offset=bass.IndirectOffsetOnAxis(ap=token[:, e:e + 1], axis=0),
                                    in_=y_sb[:, :], in_offset=None, bounds_check=T - 1,
                                    compute_op=ALU.add).then_inc(y_out, 16)
            pool.wait_ge(y_out, 16 * (e + 1))
            pool.sem_inc(y_free, 1)

    moe.close()
    perm.close()


def constants():
    ident = np.eye(P, dtype=np.float32)
    j, i = np.arange(P)[:, None], np.arange(P)[None, :]
    masks = np.zeros((P, NL, P), np.float32)
    for l, m in enumerate(LEVELS):
        masks[:, l, :] = (j // (2 * m) == i // (2 * m)) & (j // m != i // m)
    half = QK_DIM // 8
    inv_freq = (1.0 / (500000.0 ** (np.arange(0, 2 * half, 2, dtype=np.float32) / (2 * half)))).astype(np.float32)
    position = np.concatenate([np.arange(PROMPT), np.arange(SAMPLE)]).astype(np.float32)
    angle = (position[:, None] * inv_freq[None, :]).reshape(TILES, P, half).transpose(1, 0, 2)
    return ident, masks, np.ascontiguousarray(np.cos(angle)), np.ascontiguousarray(np.sin(angle))


def kernel(**inputs):
    import concourse.bacc as bacc
    from concourse.bass_utils import run_bass_kernel_spmd

    nc = bacc.Bacc("TRN2", target_bir_lowering=False, num_devices=1)
    ident, masks, cos, sin = constants()
    given = {k: np.asarray(v) for k, v in inputs.items()}
    arrays = {
        "x": np.concatenate([given["x_prompt"][0], given["x_sample"][0]], axis=0),
        "norm1": given["norm1_w"], "w_in": given["w_in"][0],
        "lbf": given["hg_lb_fwd"], "lbb": given["hg_lb_bwd"], "hgw": given["hg_norm_w"],
        "qw": given["q_norm_w"], "kw": given["k_norm_w"],
        "lams": np.concatenate([given[f"lambda_{n}"] for n in ("q1", "k1", "q2", "k2")], axis=0)[None],
        "subw": given["subln_w"], "w_out": given["w_out"][0], "norm2": given["norm2_w"],
        "rw": given["router_w"][0], "w1": given["w1"][0], "w3": given["w3"][0], "w2": given["w2"][0],
        "ident_c": ident, "masks_c": masks, "cos_c": cos, "sin_c": sin,
    }
    arrays = {k: np.ascontiguousarray(v) for k, v in arrays.items()}
    aps = [nc.dram_tensor(n, a.shape, mybir.dt.from_np(a.dtype), kind="ExternalInput").ap() for n, a in arrays.items()]
    flat = {"norm1", "hgw", "qw", "kw", "subw", "norm2"}
    aps = [ap[0, :] if n in flat else ap[0] if n == "lams" else ap for n, ap in zip(arrays, aps)]
    out = nc.dram_tensor("y", (T, D), F32, kind="ExternalOutput").ap()
    tm_d = nc.dram_tensor("projected", (T, 5 * HW), F32).ap()
    xt_d = nc.dram_tensor("moe_rows", (T, D), F32).ap()
    build(nc, *aps, out, tm_d, xt_d)
    y = run_bass_kernel_spmd(nc, [arrays], core_ids=[0]).results[0]["y"]
    return y[None, :PROMPT], y[None, PROMPT:]
```
